# Optimizing a Trainium2 kernel written in Bass

```python
import math
import jax, jax.numpy as jnp
from jax import lax
import numpy as np

D_MODEL = 1024
BATCH = 1
SEQ = 256
DEPTH = 2
DEC_BATCH = 8
DEC_SEQ = 16
PAST_LEN = 128

CHUNK = 64
Q_BLOCK = 128
N_EVEN = (DEPTH + 1) // 2
N_ODD = DEPTH // 2
FOX_HEADS = 8
FOX_HD = 64
RET_HEADS = 4
RET_DK = 64
RET_DV = 128
ROPE_BASE = 10000.0
CONV_W = 31
CONV_CH = D_MODEL
N_GROUPS = 4
EXP_PER_GROUP = 8
TOP_K = 2
D_EXPERT = 256
EPS = 1e-6

FOX_W = FOX_HEADS * FOX_HD
RET_QK_W = RET_HEADS * RET_DK
RET_V_W = RET_HEADS * RET_DV
MIX_IN = 3 * FOX_W + FOX_HEADS + 2 * RET_QK_W + 2 * RET_V_W
MIX_OUT = FOX_W + RET_V_W

kernel_name = "hybrid_stream_encoder_step"

F32 = jnp.float32

def rms_norm(x, g):
    xf = x.astype(F32)
    y = xf * lax.rsqrt(jnp.mean(xf * xf, axis=-1, keepdims=True) + EPS)
    return (y * g.astype(F32)).astype(x.dtype)

def layer_norm(x, g, b):
    xf = x.astype(F32)
    mu = jnp.mean(xf, axis=-1, keepdims=True)
    var = jnp.mean(jnp.square(xf - mu), axis=-1, keepdims=True)
    y = (xf - mu) * lax.rsqrt(var + EPS) * g.astype(F32) + b.astype(F32)
    return y.astype(x.dtype)

def rotary(x, pos):
    half = x.shape[-1] // 2
    inv_freq = ROPE_BASE ** (-jnp.arange(half, dtype=F32) / half)
    ang = pos.astype(F32)[:, None] * inv_freq[None, :]
    cos = jnp.cos(ang)[None, :, None, :]
    sin = jnp.sin(ang)[None, :, None, :]
    xf = x.astype(F32)
    x1, x2 = xf[..., :half], xf[..., half:]
    return jnp.concatenate([x1 * cos - x2 * sin, x1 * sin + x2 * cos], axis=-1).astype(x.dtype)

def retention_log_gamma():
    return jnp.log(1.0 - 2.0 ** (-5.0 - jnp.arange(RET_HEADS, dtype=F32)))

def even_projections(h, w_in, b_f, q_gain, k_gain, pos):
    B, T, _ = h.shape
    proj = jnp.einsum('btd,de->bte', h, w_in)
    sizes = [FOX_W, FOX_W, FOX_W, FOX_HEADS, RET_QK_W, RET_QK_W, RET_V_W, RET_V_W]
    cuts = [int(c) for c in np.cumsum(sizes)[:-1]]
    fq, fk, fv, ff, rq, rk, rv, rg = jnp.split(proj, cuts, axis=-1)
    fq = rms_norm(fq.reshape(B, T, FOX_HEADS, FOX_HD), q_gain)
    fk = rms_norm(fk.reshape(B, T, FOX_HEADS, FOX_HD), k_gain)
    fv = fv.reshape(B, T, FOX_HEADS, FOX_HD)
    logf = jax.nn.log_sigmoid(ff.astype(F32) + b_f.astype(F32))
    rq = rotary(rq.reshape(B, T, RET_HEADS, RET_DK), pos)
    rk = rotary(rk.reshape(B, T, RET_HEADS, RET_DK), pos) * (RET_DK ** -0.5)
    rv = rv.reshape(B, T, RET_HEADS, RET_DV)
    return fq, fk, fv, logf, rq, rk, rv, rg

def fox_attend(q, k, v, cq, ck, qpos, kpos):
    s = jnp.einsum('bqhd,bkhd->bhqk', q.astype(F32), k.astype(F32)) * (q.shape[-1] ** -0.5)
    s = s + cq[..., :, None] - ck[..., None, :]
    s = jnp.where(kpos[None, :] <= qpos[:, None], s, -jnp.inf)
    p = jax.nn.softmax(s, axis=-1)
    return jnp.einsum('bhqk,bkhd->bqhd', p, v.astype(F32)).astype(q.dtype)

def fox_prompt(q, k, v, logf):
    B, T, H, d = q.shape
    nb = T // Q_BLOCK
    cT = jnp.cumsum(logf, axis=1).transpose(0, 2, 1)
    qb = q.reshape(B, nb, Q_BLOCK, H, d).transpose(1, 0, 2, 3, 4)
    cqb = cT.reshape(B, H, nb, Q_BLOCK).transpose(2, 0, 1, 3)
    kpos = jnp.arange(T)

    def one_block(args):
        qi, cqi, bi = args
        qpos = bi * Q_BLOCK + jnp.arange(Q_BLOCK)
        return fox_attend(qi, k, v, cqi, cT, qpos, kpos)

    out = lax.map(one_block, (qb, cqb, jnp.arange(nb)))
    return out.transpose(1, 0, 2, 3, 4).reshape(B, T, H, d)

def fox_sample(q, k_all, v_all, logf_all):
    L = q.shape[1]
    P = k_all.shape[1] - L
    cT = jnp.cumsum(logf_all, axis=1).transpose(0, 2, 1)
    qpos = P + jnp.arange(L)
    kpos = jnp.arange(P + L)
    return fox_attend(q, k_all, v_all, cT[:, :, P:], cT, qpos, kpos)

def retention_block(q, k, v, s_prev, log_gamma):
    L = q.shape[1]
    idx = jnp.arange(L, dtype=F32)
    diff = idx[:, None] - idx[None, :]
    decay = jnp.where(diff >= 0, jnp.exp(log_gamma[:, None, None] * jnp.maximum(diff, 0.0)), 0.0)
    qf, kf, vf = q.astype(F32), k.astype(F32), v.astype(F32)
    scores = jnp.einsum('blhd,bmhd->bhlm', qf, kf) * decay[None]
    inner = jnp.einsum('bhlm,bmhe->blhe', scores, vf)
    cross = jnp.einsum('blhd,bhde->blhe', qf, s_prev) * jnp.exp(log_gamma[None, :] * (idx[:, None] + 1.0))[None, :, :, None]
    k_dec = kf * jnp.exp(log_gamma[None, :] * (L - 1.0 - idx)[:, None])[None, :, :, None]
    s_new = jnp.exp(log_gamma * L)[None, :, None, None] * s_prev + jnp.einsum('blhd,blhe->bhde', k_dec, vf)
    return inner + cross, s_new

def retention_prompt(q, k, v, log_gamma):
    B, T, H, dk = q.shape
    dv = v.shape[-1]
    nc = T // CHUNK

    def to_chunks(a):
        return a.reshape(B, nc, CHUNK, *a.shape[2:]).swapaxes(0, 1)

    def step(s, inp):
        qc, kc, vc = inp
        o, s = retention_block(qc, kc, vc, s, log_gamma)
        return s, o

    s0 = jnp.zeros((B, H, dk, dv), F32)
    s_fin, o = lax.scan(step, s0, (to_chunks(q), to_chunks(k), to_chunks(v)))
    return o.swapaxes(0, 1).reshape(B, T, H, dv), s_fin

def ret_head_norm(y, g):
    mu = jnp.mean(y, axis=-1, keepdims=True)
    var = jnp.mean(jnp.square(y - mu), axis=-1, keepdims=True)
    return (y - mu) * lax.rsqrt(var + EPS) * g.reshape(RET_HEADS, RET_DV).astype(F32)

def even_output(o_fox, y_ret, rg, gn_gain, w_out):
    B, T = o_fox.shape[:2]
    o_ret = jax.nn.silu(rg.astype(F32)) * ret_head_norm(y_ret, gn_gain).reshape(B, T, RET_V_W)
    o = jnp.concatenate([o_fox.reshape(B, T, FOX_W), o_ret.astype(o_fox.dtype)], axis=-1)
    return jnp.einsum('bte,ed->btd', o, w_out)

def conv_glu(h, w_pw1, b_pw1):
    a, g = jnp.split(jnp.einsum('btd,dc->btc', h, w_pw1) + b_pw1, 2, axis=-1)
    return a * jax.nn.sigmoid(g)

def conv_rest(u_ext, w_dw, b_dw, ln_g, ln_b, w_pw2):
    y = lax.conv_general_dilated(u_ext, w_dw[:, None, :], window_strides=(1,), padding='VALID',
                                 dimension_numbers=('NWC', 'WIO', 'NWC'),
                                 feature_group_count=CONV_CH) + b_dw
    y = jax.nn.silu(layer_norm(y, ln_g, ln_b))
    return jnp.einsum('btc,cd->btd', y, w_pw2)

def hier_moe(h, w_grp, b_grp, w_rexp, b_rexp, w_gate, w_up, w_down):
    B, T, D = h.shape
    x = h.reshape(B * T, D)
    g_logits = jnp.einsum('nd,dg->ng', x, w_grp).astype(F32) + b_grp.astype(F32)
    grp = jnp.argmax(g_logits, axis=-1)
    p_grp = jnp.take_along_axis(jax.nn.softmax(g_logits, axis=-1), grp[:, None], axis=-1)
    e_logits = (jnp.einsum('nd,de->ne', x, w_rexp).astype(F32) + b_rexp.astype(F32)).reshape(B * T, N_GROUPS, EXP_PER_GROUP)
    e_sel = jnp.take_along_axis(e_logits, grp[:, None, None], axis=1)[:, 0]
    top_v, top_i = lax.top_k(e_sel, TOP_K)
    top_w = jax.nn.softmax(top_v, axis=-1) * p_grp
    w_in_grp = jnp.einsum('nk,nke->ne', top_w, jax.nn.one_hot(top_i, EXP_PER_GROUP, dtype=F32))
    gates = (jax.nn.one_hot(grp, N_GROUPS, dtype=F32)[:, :, None] * w_in_grp[:, None, :]).astype(x.dtype)
    out = jnp.zeros((B * T, D), F32)
    for g in range(N_GROUPS):
        a = jnp.einsum('nd,edf->nef', x, w_gate[g])
        u = jnp.einsum('nd,edf->nef', x, w_up[g])
        hid = jax.nn.silu(a) * u * gates[:, g, :, None]
        out = out + jnp.einsum('nef,efd->nd', hid, w_down[g]).astype(F32)
    return out.astype(h.dtype).reshape(B, T, D)

def setup_inputs(seed: int = 0) -> dict:
    key = jax.random.key(seed)
    ks = list(jax.random.split(key, 32))

    def nrm(i, shape, scale):
        return scale * jax.random.normal(ks[i], shape, F32)

    return {
        'x_prompt': nrm(0, (BATCH, SEQ, D_MODEL), 1.0),
        'x_sample': nrm(1, (DEC_BATCH, DEC_SEQ, D_MODEL), 1.0),
        'cache_fox_k': nrm(2, (N_EVEN, DEC_BATCH, PAST_LEN, FOX_HEADS, FOX_HD), 1.0),
        'cache_fox_v': nrm(3, (N_EVEN, DEC_BATCH, PAST_LEN, FOX_HEADS, FOX_HD), 1.0),
        'cache_fox_logf': jax.nn.log_sigmoid(2.0 + nrm(4, (N_EVEN, DEC_BATCH, PAST_LEN, FOX_HEADS), 1.0)),
        'state_ret': nrm(5, (N_EVEN, DEC_BATCH, RET_HEADS, RET_DK, RET_DV), 0.5),
        'cache_conv': nrm(6, (N_ODD, DEC_BATCH, CONV_W - 1, CONV_CH), 0.5),
        'norm_mix': 1.0 + nrm(7, (DEPTH, D_MODEL), 0.02),
        'norm_ffn': 1.0 + nrm(8, (DEPTH, D_MODEL), 0.02),
        'w_in_mix': nrm(9, (N_EVEN, D_MODEL, MIX_IN), D_MODEL ** -0.5),
        'b_forget': 2.0 + nrm(10, (N_EVEN, FOX_HEADS), 0.5),
        'fox_q_gain': 1.0 + nrm(11, (N_EVEN, FOX_HD), 0.02),
        'fox_k_gain': 1.0 + nrm(12, (N_EVEN, FOX_HD), 0.02),
        'ret_gn_gain': 1.0 + nrm(13, (N_EVEN, RET_V_W), 0.02),
        'w_out_mix': nrm(14, (N_EVEN, MIX_OUT, D_MODEL), MIX_OUT ** -0.5),
        'w_pw1': nrm(15, (N_ODD, D_MODEL, 2 * CONV_CH), D_MODEL ** -0.5),
        'b_pw1': nrm(16, (N_ODD, 2 * CONV_CH), 0.02),
        'w_dw': nrm(17, (N_ODD, CONV_W, CONV_CH), CONV_W ** -0.5),
        'b_dw': nrm(18, (N_ODD, CONV_CH), 0.02),
        'conv_ln_g': 1.0 + nrm(19, (N_ODD, CONV_CH), 0.02),
        'conv_ln_b': nrm(20, (N_ODD, CONV_CH), 0.02),
        'w_pw2': nrm(21, (N_ODD, CONV_CH, D_MODEL), CONV_CH ** -0.5),
        'w_router_group': nrm(22, (DEPTH, D_MODEL, N_GROUPS), D_MODEL ** -0.5),
        'b_router_group': nrm(23, (DEPTH, N_GROUPS), 0.01),
        'w_router_expert': nrm(24, (DEPTH, D_MODEL, N_GROUPS * EXP_PER_GROUP), D_MODEL ** -0.5),
        'b_router_expert': nrm(25, (DEPTH, N_GROUPS * EXP_PER_GROUP), 0.01),
        'w_exp_gate': nrm(26, (DEPTH, N_GROUPS, EXP_PER_GROUP, D_MODEL, D_EXPERT), D_MODEL ** -0.5),
        'w_exp_up': nrm(27, (DEPTH, N_GROUPS, EXP_PER_GROUP, D_MODEL, D_EXPERT), D_MODEL ** -0.5),
        'w_exp_down': nrm(28, (DEPTH, N_GROUPS, EXP_PER_GROUP, D_EXPERT, D_MODEL), D_EXPERT ** -0.5),
    }

def reference(x_prompt, x_sample, cache_fox_k, cache_fox_v, cache_fox_logf, state_ret, cache_conv,
              norm_mix, norm_ffn, w_in_mix, b_forget, fox_q_gain, fox_k_gain, ret_gn_gain, w_out_mix,
              w_pw1, b_pw1, w_dw, b_dw, conv_ln_g, conv_ln_b, w_pw2,
              w_router_group, b_router_group, w_router_expert, b_router_expert,
              w_exp_gate, w_exp_up, w_exp_down):
    xp, xs = x_prompt, x_sample
    T = xp.shape[1]
    L = xs.shape[1]
    P = cache_fox_k.shape[2]
    pos_p = jnp.arange(T)
    pos_s = P + jnp.arange(L)
    log_gamma = retention_log_gamma()

    fk_p, fv_p, lf_p, rs_p, cv_p = [], [], [], [], []
    fk_s, fv_s, lf_s, rs_s, cv_s = [], [], [], [], []

    for l in range(DEPTH):
        i = l // 2
        hp = rms_norm(xp, norm_mix[l])
        hs = rms_norm(xs, norm_mix[l])
        if l % 2 == 0:
            fq, fk, fv, logf, rq, rk, rv, rg = even_projections(hp, w_in_mix[i], b_forget[i], fox_q_gain[i], fox_k_gain[i], pos_p)
            o_fox = fox_prompt(fq, fk, fv, logf)
            y_ret, s_fin = retention_prompt(rq, rk, rv, log_gamma)
            xp = xp + even_output(o_fox, y_ret, rg, ret_gn_gain[i], w_out_mix[i])
            fk_p.append(fk); fv_p.append(fv); lf_p.append(logf); rs_p.append(s_fin)
            sq, sk, sv, slogf, srq, srk, srv, srg = even_projections(hs, w_in_mix[i], b_forget[i], fox_q_gain[i], fox_k_gain[i], pos_s)
            k_all = jnp.concatenate([cache_fox_k[i].astype(sk.dtype), sk], axis=1)
            v_all = jnp.concatenate([cache_fox_v[i].astype(sv.dtype), sv], axis=1)
            lf_all = jnp.concatenate([cache_fox_logf[i].astype(F32), slogf], axis=1)
            o_fox_s = fox_sample(sq, k_all, v_all, lf_all)
            y_ret_s, s_new = retention_block(srq, srk, srv, state_ret[i].astype(F32), log_gamma)
            xs = xs + even_output(o_fox_s, y_ret_s, srg, ret_gn_gain[i], w_out_mix[i])
            fk_s.append(sk); fv_s.append(sv); lf_s.append(slogf); rs_s.append(s_new)
        else:
            up = conv_glu(hp, w_pw1[i], b_pw1[i])
            up_ext = jnp.pad(up, ((0, 0), (CONV_W - 1, 0), (0, 0)))
            xp = xp + conv_rest(up_ext, w_dw[i], b_dw[i], conv_ln_g[i], conv_ln_b[i], w_pw2[i])
            cv_p.append(up[:, T - (CONV_W - 1):])
            us = conv_glu(hs, w_pw1[i], b_pw1[i])
            us_ext = jnp.concatenate([cache_conv[i].astype(us.dtype), us], axis=1)
            xs = xs + conv_rest(us_ext, w_dw[i], b_dw[i], conv_ln_g[i], conv_ln_b[i], w_pw2[i])
            cv_s.append(us_ext[:, L:])
        xp = xp + hier_moe(rms_norm(xp, norm_ffn[l]), w_router_group[l], b_router_group[l], w_router_expert[l],
                           b_router_expert[l], w_exp_gate[l], w_exp_up[l], w_exp_down[l])
        xs = xs + hier_moe(rms_norm(xs, norm_ffn[l]), w_router_group[l], b_router_group[l], w_router_expert[l],
                           b_router_expert[l], w_exp_gate[l], w_exp_up[l], w_exp_down[l])

    fox_k_prompt = jnp.stack(fk_p)
    fox_v_prompt = jnp.stack(fv_p)
    fox_logf_prompt = jnp.stack(lf_p)
    ret_state_prompt = jnp.stack(rs_p)
    conv_prompt = jnp.stack(cv_p)
    fox_k_sample = jnp.stack(fk_s)
    fox_v_sample = jnp.stack(fv_s)
    fox_logf_sample = jnp.stack(lf_s)
    ret_state_sample = jnp.stack(rs_s)
    conv_sample = jnp.stack(cv_s)
    return (xp, xs, fox_k_prompt, fox_v_prompt, fox_logf_prompt, ret_state_prompt, conv_prompt,
            fox_k_sample, fox_v_sample, fox_logf_sample, ret_state_sample, conv_sample)


_drawn_inputs = setup_inputs


def setup_inputs(seed=0):
    import zlib

    import numpy as np

    out = dict(_drawn_inputs(seed))
    spreads = {}
    factors = {'fox_q_gain': 3.047, 'fox_k_gain': 3.114, 'conv_ln_b': 4.158}
    for name, (base, spread) in spreads.items():
        noise = np.random.default_rng([zlib.crc32(name.encode()), seed]).standard_normal(out[name].shape)
        drawn = base * np.exp(spread * noise) if base else spread * noise
        out[name] = __import__('jax').numpy.asarray(drawn.astype(out[name].dtype))
    for name, factor in factors.items():
        out[name] = (out[name] * factor).astype(out[name].dtype)
    return out
```

```python
from contextlib import ExitStack

import numpy as np

import concourse.bass as bass
from concourse import mybir

F32 = mybir.dt.float32
F32R = mybir.dt.float32r
I32 = mybir.dt.int32
ALU = mybir.AluOpType
ACT = mybir.ActivationFunctionType
AXX = mybir.AxisListType.X

P = 128
D = 1024
KD = D // P
NT = 3
TOK = NT * P
SEQ, NS, LS, PAST = 256, 8, 16, 128
FH, FD = 8, 64
RH, RK, RV = 4, 64, 128
MIX = 3 * FH * FD + 2 * RH * RK + 2 * RH * RV
QO, KO, VO = 0, FH * FD, 2 * FH * FD
FF_COL = 3 * FH * FD
RQO = 3 * FH * FD
RVO = RQO + 2 * RH * RK
RGO = RVO + RH * RV
KEYS = PAST + LS
CONV_W, HIST = 31, 30
NG, EPG, NE, FE = 4, 8, 32, 256
NR = NG + NE
CAP = 64
QUAD = 4
NQ = NE // QUAD
MAXWIN = TOK // CAP
EPS = 1e-6
MIX_LOADS = 6 + NS
STATE_STORES = 1 + NS
CONV_STORES = 1 + NS
NEG = -1e30
UNIT = 2048
LO, HI = 6, 12
UCOL = 256


def gammas():
    return 1.0 - 2.0 ** (-5.0 - np.arange(RH, dtype=np.float64))


def layout(parts):
    at, n = {}, 0
    for name, width in parts:
        at[name] = (n, n + width)
        n += width
    return at, n


CONSTS, CONST_W = layout([
    ("ident", P), ("tri", P), ("strict", P), ("ones", P), ("blk", P), ("mask", 2 * P), ("smask", KEYS),
    ("rowpar", 2), ("sel", P + P - LS), ("cos", NT * 32), ("sin", NT * 32), ("iota", CAP), ("tie", EPG),
    ("onesd", P), ("eps", 1)])
RCONSTS, RCONST_W = layout([
    ("dec_p", RH * P), ("dec_s", RH * P), ("kdec_p", RH), ("kdec_s", 2 * RH), ("qdec_p", RH * P),
    ("qdec_s", RH * P)])


def constants():
    p = np.arange(P)
    c = np.zeros((P, CONST_W), np.float64)

    def put(name, a):
        a0, a1 = CONSTS[name]
        c[:, a0:a1] = np.asarray(a, np.float64).reshape(P, a1 - a0)

    k, m = p[:, None], p[None, :]
    put("ident", k == m)
    put("tri", k <= m)
    put("strict", k < m)
    put("ones", np.ones((P, P)))
    put("blk", (k <= m) & (k // LS == m // LS))
    put("mask", np.concatenate([np.zeros((P, P)), np.where(m <= k, 0.0, NEG)], 1))
    j = np.arange(KEYS)[None, :]
    put("smask", np.where((j < PAST) | (j - PAST <= k % LS), 0.0, NEG))
    par = (p // LS) % 2
    put("rowpar", np.stack([par == 0, par == 1], 1))
    sel = np.zeros((P, P + P - LS))
    sel[:, P - LS:P] = 1.0
    put("sel", sel)
    pos = np.stack([p, P + p, PAST + p % LS], 1).astype(np.float32)
    freq = (np.float32(10000.0) ** (-np.arange(32, dtype=np.float32) / np.float32(32))).astype(np.float32)
    ang = (pos[:, :, None] * freq[None, None, :]).astype(np.float32).astype(np.float64)
    put("cos", np.cos(ang))
    put("sin", np.sin(ang))
    put("iota", np.broadcast_to(np.arange(CAP), (P, CAP)))
    put("tie", np.broadcast_to(EPG - np.arange(EPG), (P, EPG)))
    put("onesd", np.full((P, P), 1.0 / D))
    put("eps", np.full((P, 1), EPS))
    g = gammas()
    r = np.zeros((P, RCONST_W), np.float64)

    def putr(name, a):
        a0, a1 = RCONSTS[name]
        r[:, a0:a1] = np.asarray(a, np.float64).reshape(P, a1 - a0)

    diff = np.maximum(m - k, 0)
    idx = p % LS
    putr("dec_p", np.stack([np.where(k <= m, gg ** diff, 0.0) for gg in g], 1))
    putr("dec_s", np.stack([np.where((k <= m) & (k // LS == m // LS), gg ** diff, 0.0) for gg in g], 1))
    putr("kdec_p", np.stack([gg ** (P - 1.0 - p) for gg in g], 1))
    putr("kdec_s", np.stack([np.where(par == q, gg ** (LS - 1.0 - idx), 0.0) for gg in g for q in (0, 1)], 1))
    putr("qdec_p", np.broadcast_to(np.stack([gg ** (p + 1.0) for gg in g], 0)[None], (P, RH, P)))
    half = (p // RK)[:, None, None]
    putr("qdec_s", np.where(par[None, None, :] == half, np.stack([gg ** (idx + 1.0) for gg in g], 0)[None], 0.0))
    head = np.zeros((FH, FH, TOK))
    for h in range(FH):
        head[h, h] = 1.0
    return c.astype(np.float32), r.astype(np.float32), head.reshape(FH, FH * TOK).astype(np.float32)


class InOrder:

    def __init__(self, eng, own):
        self.eng, self.own, self.count, self.open = eng, own, {}, {}

    def do(self, ins, sem=None):
        sem = self.own if sem is None else sem
        n = self.count.get(id(sem), 0) + 1
        self.count[id(sem)] = n
        self.open[id(sem)] = (sem, n)
        ins.then_inc(sem, 1)

    def settle(self):
        for sem, n in self.open.values():
            self.eng.wait_ge(sem, n)
        self.open = {}

    def link(self, ins, sem=None):
        self.do(ins, sem)
        self.settle()


def bc(ap, dim, n):
    shape = list(ap.shape)
    return ap.unsqueeze(dim).to_broadcast(shape[:dim] + [n] + shape[dim:])


def build(nc, a, o):
    with ExitStack() as ctx:
        sems = {}

        def S(name):
            if name not in sems:
                sems[name] = ctx.enter_context(nc.semaphore(name))
            return sems[name]

        class Region:
            def __init__(self, start, end):
                self.n, self.end = start, end

            def __call__(self, name, shape, dt=F32):
                off = self.n
                self.n += (int(np.prod(shape[1:])) * 4 + 31) // 32 * 32
                assert self.n <= self.end, (name, self.n, self.end)
                return nc.alloc_sbuf_tensor_at(name, shape, dt, offset=off)

        limit = nc.sbuf_usable_end // 32 * 32
        keep = Region((nc.sbuf_base + 31) // 32 * 32, limit)
        X = keep("X", [P, NT, D])
        cst = keep("cst", [P, CONST_W])
        gb = keep("gain_rows", [P, D])
        stat = keep("stat", [P, 16])
        NW = keep("steps", [P, 8], I32)
        slot = [keep(f"slot{i}", [P, UNIT]) for i in range(LO)]
        hi_at = keep.n
        slot += [keep(f"slot{i}", [P, UNIT]) for i in range(LO, HI)]
        arena = keep.n
        C = {n: cst[:, x0:x1] for n, (x0, x1) in CONSTS.items()}
        ident = C["ident"]

        rh = Region(hi_at, arena)
        PJ = rh("PJ", [P, NT, MIX])
        STt = rh("STt", [P, 4, RH, RV])
        FF = rh("FF", [P, NT, FH])
        LF = rh("LF", [P, NT, FH])
        LT = rh("LT", [P, NT, FH])
        CQ = rh("CQ", [P, NT, FH])
        CLF = rh("CLF", [P, NS, FH])
        WF = rh("WF", [P, KD, FH])
        GQ = rh("GQ", [P, FD])
        GK = rh("GK", [P, FD])
        BF = rh("BF", [P, FH])
        MS = rh("MS", [P, NT * FH])
        MX = rh("MX", [P, 16])
        SM = rh("SM", [P, 16])
        RR = rh("RR", [P, 16])
        ra = Region(arena, limit)
        HT = ra("HT", [P, KD, TOK])
        QT = ra("QT", [P, FH, TOK])
        KT = ra("KT", [P, FH, TOK])
        over = Region(ra.n, limit)
        HN = over("HN", [P, NT, D])
        SQ = over("SQ", [P, NT, FH * FD])
        over = Region(ra.n, limit)
        PN = over("PN", [P, FH, P])
        KTC = ra("KTC", [P, NS, FH, KEYS])
        over = Region(ra.n, limit)
        SS = over("SS", [P, 2, TOK])
        ES = ra("ES", [P, FH * 2, KEYS])
        PT = ra("PT", [P, 2, TOK])
        over = Region(arena, limit)
        YQ = over("YQ", [P, NT, RH, RV])
        rr = Region(arena + TOK * KD * 4, limit)
        rcst = rr("rcst", [P, RCONST_W])
        RT = rr("RT", [P, NT, 2 * RH, RK])
        T1 = rr("T1", [P, NT, 2 * RH, RK // 2])
        T2 = rr("T2", [P, NT, 2 * RH, RK // 2])
        QRT = rr("QRT", [P, 2 * RH, TOK])
        SD = rr("SD", [P, 2, TOK])
        QD1 = rr("QD1", [P, RH, P])
        QD2 = rr("QD2", [P, RH, P])
        KDP = rr("KDP", [P, 2, RH, RK])
        KDS = rr("KDS", [P, RH, 2, RK])
        S1 = rr("S1", [P, RH, 2, RV])
        STN = rr("STN", [P, 4, RH, RV])
        VM = rr("VM", [P, 4, RH * RV])
        YR = rr("YR", [P, NT, RH, RV])
        GN = rr("GN", [P, RH * RV])
        RC = {n: rcst[:, x0:x1] for n, (x0, x1) in RCONSTS.items()}

        rm = Region(arena, limit)
        XHI = rm("XHI", [P, NT, D], F32R)
        XLO = rm("XLO", [P, NT, D], F32R)
        XG = rm("XG", [P, KD, QUAD * CAP])
        G = rm("G", [P, NT * QUAD, CAP], F32R)
        GW = rm("GW", [P, NT * QUAD, CAP])
        GT = rm("GT", [P, 2, TOK], F32R)
        over = Region(rm.n, limit)
        NM = over("NM", [P, NT, D])
        YH = rm("YH", [P, 2, D], F32R)
        YL = rm("YL", [P, 2, D], F32R)
        SG = rm("SG", [P, 2, 2, 2 * CAP])
        HID = rm("HID", [P, 2, 2, 2, CAP])
        SV = rm("SV", [P, MAXWIN * NQ, NT * QUAD])
        WV = rm("WV", [P, MAXWIN * NQ, NT * QUAD])
        GATE = rm("GATE", [P, 2])
        HM = rm("HM", [P, KD, TOK])
        WR = rm("WR", [P, KD, NR])
        BR = rm("BR", [P, NR])
        LG = rm("LG", [P, NT, NR])
        OH = rm("OH", [P, NT, NG])
        E4 = rm("E4", [P, NT, NG])
        EQ = rm("EQ", [P, NT, NE])
        SE = rm("SE", [P, NT, NE])
        O1 = rm("O1", [P, NT, NE])
        O2 = rm("O2", [P, NT, NE])
        WG = rm("WG", [P, NT, NE])
        SL = rm("SL", [P, NT, NE])
        R8 = rm("R8", [P, 48])

        rc = Region(arena, limit)
        HC = rc("HC", [P, KD, TOK])
        WID = HIST + SEQ + NS * (HIST + LS)
        U = rc("U", [P, KD, WID])
        over = Region(rc.n, limit)
        NC = over("NC", [P, NT, D])
        YC = rc("YC", [P, KD, TOK])
        YS = rc("YS", [P, KD, TOK])
        SGC = rc("SGC", [P, 2, TOK])
        CC = rc("CC", [P, 2, D])
        WDR = rc("WDR", [P, D])
        WDT = rc("WDT", [P, KD, CONV_W])
        SMR = rc("SMR", [P, P])
        SMT = rc("SMT", [P, 40])
        CS = rc("CS", [P, D])
        CP = rc("CP", [P, D])
        VR = rc("VR", [P, TOK])

        PS = nc.alloc_psum_tensor("PS", [P, 8, 512], F32)

        xp = a["x_prompt"].rearrange("b (t p) d -> p (b t) d", p=P)
        xs = a["x_sample"].rearrange("b l d -> (b l) d")
        w_in = a["w_in_mix"].rearrange("l (p k) n -> p (l k) n", k=KD)
        w_out = a["w_out_mix"].rearrange("l (p k) n -> p (l k) n", k=KD)
        w_pw1 = a["w_pw1"].rearrange("l (p k) n -> p (l k) n", k=KD)
        w_pw2 = a["w_pw2"].rearrange("l (k p) n -> p (l k) n", k=KD)
        w_gate = a["w_exp_gate"].rearrange("l g e (p k) f -> (l g e) p (k f)", k=KD)
        w_up = a["w_exp_up"].rearrange("l g e (p k) f -> (l g e) p (k f)", k=KD)
        w_down = a["w_exp_down"].rearrange("l g e (j p) n -> (l g e) p j n", p=P)

        def row(ap, n):
            return ap.rearrange("(o n) -> o n", o=1).to_broadcast([P, n])

        def cols(u):
            return UCOL * u + (FH if u >= FF_COL // UCOL else 0)

        def dense(i):
            return slot[i % LO][:, :].rearrange("p (k n) -> p k n", k=KD)

        N_IN = MIX // UCOL
        block = ctx.enter_context(nc.Block())

        @block.sync
        def _(sp):
            for t in range(2):
                sp.dma_start(X[:, t, :], xp[:, t, :]).then_inc(S("x_in"), 16)
            sp.dma_start(X[:, 2, :], xs).then_inc(S("x_in"), 16)
            sp.dma_start(gb[:, :], row(a["norm_mix"][0], D)).then_inc(S("x_in"), 16)
            sp.dma_start(cst[:, :], a["cst"]).then_inc(S("cst_in"), 16)

            def unit(seg, i):
                return dense(i), S(f"{seg}_full{i % LO}")

            for i in range(N_IN):
                if i >= LO:
                    sp.wait_ge(S("proj_done"), i - LO + 1)
                dst, full = unit("a", i)
                sp.dma_start(dst, w_in[:, :, cols(i):cols(i) + UCOL]).then_inc(full, 16)
            for i in range(4):
                sp.wait_ge(S("proj_done"), LO + i + 1)
                src = a["cache_fox_k" if i < 2 else "cache_fox_v"]
                src = src[0, 4 * (i % 2):4 * (i % 2) + 4].rearrange("b p h d -> p b (h d)")
                n = N_IN + i
                sp.dma_start(slot[n % LO][:, :].rearrange("p (b c) -> p b c", b=4), src).then_inc(
                    S(f"a_full{n % LO}"), 16)
            for i in range(4):
                if i < 2:
                    sp.wait_ge(S("proj_done"), N_IN - 1 + i)
                else:
                    sp.wait_ge(S("cachek_tr"), 4 * (i - 1))
                dst, full = unit("a", N_IN + 4 + i)
                sp.dma_start(dst, w_out[:, :, UCOL * i:UCOL * i + UCOL]).then_inc(full, 16)

            def expert_loads(lay, q, before):
                for pair in range(2):
                    for e in range(2):
                        for half in range(2):
                            n = 6 * pair + 2 * e + half
                            before(n)
                            src = (w_gate, w_up)[half][bass.ds(q * QUAD + (lay * NE + 2 * pair + e), 1)]
                            sp.dma_start(slot[n][:, :], src.rearrange("o p n -> p (o n)")).then_inc(
                                S(f"gu_full{2 * pair + e}"), 16)
                    for e in range(2):
                        n = 6 * pair + 4 + e
                        before(n)
                        src = w_down[bass.ds(q * QUAD + (lay * NE + 2 * pair + e), 1)]
                        sp.dma_start(slot[n][:, :].rearrange("p (j n) -> p j n", j=2),
                                     src.rearrange("o p j n -> p (o j) n")).then_inc(
                            S(f"d_full{2 * pair + e}"), 16)

            def expert_loop(lay, base, n):
                with sp.Fori(base + 1, base + n) as s:
                    def before(j):
                        pair, k = divmod(j, 6)
                        if k < 4:
                            sp.wait_ge(S(f"gu_done"), s * 4 + (2 * pair + k // 2 - 3))
                        else:
                            sp.wait_ge(S(f"d_done"), s * 4 + (2 * pair + k - 4 - 3))
                    expert_loads(lay, s % NQ, before)

            def first_a(n):
                if n < 2:
                    sp.wait_ge(S("wout_done"), 3 + n)
                elif n < 4:
                    sp.wait_ge(S("cachev_used"), 1)
                elif n < LO:
                    sp.wait_ge(S("wout_done"), n - 3)
                else:
                    sp.wait_ge(S("tr_done"), 2 * KD)
                    sp.wait_ge(S("mix_stored"), 16 * 5)
            expert_loads(0, 0, first_a)
            sp.wait_ge(S("steps_known"), 1)
            n0 = sp.value_load(NW[0:1, 0:1], min_val=0, max_val=(MAXWIN - 1) * NQ) + NQ
            expert_loop(0, 0, n0)

            def after_moe(j):
                pair, k = divmod(j, 6)
                if k < 4:
                    sp.wait_ge(S("gu_done"), n0 * 4 + (2 * pair + k // 2 - 3))
                else:
                    sp.wait_ge(S("d_done"), n0 * 4 + (2 * pair + k - 4 - 3))

            for i in range(12):
                if i < LO:
                    after_moe(i)
                else:
                    sp.wait_ge(S("pw_done"), i - LO + 1)
                dst, full = unit("c", i)
                if i < 8:
                    c0 = D * (i % 2) + UCOL * (i // 2)
                    sp.dma_start(dst, w_pw1[:, :, c0:c0 + UCOL]).then_inc(full, 16)
                else:
                    sp.dma_start(dst, w_pw2[:, :, UCOL * (i - 8):UCOL * (i - 7)]).then_inc(full, 16)

            def first_c(n):
                if n < LO:
                    sp.wait_ge(S("pw_done"), LO + n + 1)
                else:
                    after_moe(n)
            expert_loads(1, 0, first_c)
            sp.wait_ge(S("steps_known"), 2)
            n1 = sp.value_load(NW[0:1, 1:2], min_val=0, max_val=(MAXWIN - 1) * NQ) + NQ
            expert_loop(1, n0, n1)

        @block.gpsimd
        def _(pool):
            for dst, src in ((CLF[:, :, :], a["cache_fox_logf"][0].rearrange("b p h -> p b h")),
                             (WF[:, :, :], w_in[:, :, FF_COL:FF_COL + FH]),
                             (GQ[:, :], row(a["fox_q_gain"][0], FD)), (GK[:, :], row(a["fox_k_gain"][0], FD)),
                             (BF[:, :], row(a["b_forget"][0], FH)),
                             (QT[FD:FD + FH, :, :], a["head"].rearrange("c (h t) -> c h t", h=FH))):
                pool.dma_start(dst, src).then_inc(S("mix_in"), 16)
            for b in range(NS):
                pool.dma_start(STt[RK * (b % 2):RK * (b % 2 + 1), b // 2, :, :],
                               a["state_ret"][0, b].rearrange("h d v -> d h v")).then_inc(S("mix_in"), 16)

            def store(dst, src, sem="stored"):
                pool.dma_start(dst, src).then_inc(S(sem), 16)

            tiles = "b (t p) h d -> p (b t) (h d)"
            flat = "b l h d -> (b l) (h d)"
            pool.wait_ge(S("k_ready"), 1)
            store(o["fox_k_prompt"][0].rearrange(tiles, p=P), PJ[:, 0:2, KO:VO], "k_stored")
            store(o["fox_k_sample"][0].rearrange(flat), PJ[:, 2, KO:VO], "k_stored")
            pool.wait_ge(S("lf_ready"), 1)
            store(o["fox_logf_prompt"][0].rearrange("b (t p) h -> p (b t) h", p=P), LF[:, 0:2, :], "mix_stored")
            store(o["fox_logf_sample"][0].rearrange("b l h -> (b l) h"), LF[:, 2, :], "mix_stored")
            pool.wait_ge(S("pj_ready"), N_IN)
            store(o["fox_v_prompt"][0].rearrange(tiles, p=P), PJ[:, 0:2, VO:RQO], "mix_stored")
            store(o["fox_v_sample"][0].rearrange(flat), PJ[:, 2, VO:RQO], "mix_stored")
            pool.wait_ge(S("hn_ready"), NT)
            pool.dma_start(gb[:, :], row(a["norm_ffn"][0], D)).then_inc(S("gain_in"), 16)
            pool.wait_ge(S("fox_done"), 1)
            pool.dma_start(rcst[:, :], a["rcst"]).then_inc(S("ret_in"), 16)
            pool.dma_start(GN[:, :], row(a["ret_gn_gain"][0], RH * RV)).then_inc(S("ret_in"), 16)
            nc.gpsimd.memset(VM[:, :, :], 0.0).then_inc(S("vm_zero"), 1)
            pool.wait_ge(S("s2_ready"), RH)
            store(o["ret_state_prompt"][0, 0].rearrange("h d v -> d h v"), S1[0:RK, :, 1, :])
            pool.wait_ge(S("stn_ready"), 4)
            for b in range(NS):
                store(o["ret_state_sample"][0, b].rearrange("h d v -> d h v"),
                      STN[RK * (b % 2):RK * (b % 2 + 1), b // 2, :, :])
            store(o["conv_sample"][0, :, 0:HIST - LS, :], a["cache_conv"][0, :, LS:HIST, :], "mix_stored")
            pool.wait_ge(S("stored"), 16 * STATE_STORES)
            for lay in range(2):
                pool.wait_ge(S("x_mixed"), 8 * (lay + 1))
                pool.dma_start(WR[:, :, 0:NG], a["w_router_group"][lay].rearrange("(p k) n -> p k n", k=KD)
                               ).then_inc(S("router_in"), 16)
                pool.dma_start(WR[:, :, NG:NR], a["w_router_expert"][lay].rearrange("(p k) n -> p k n", k=KD)
                               ).then_inc(S("router_in"), 16)
                pool.dma_start(BR[:, 0:NG], row(a["b_router_group"][lay], NG)).then_inc(S("router_in"), 16)
                pool.dma_start(BR[:, NG:NR], row(a["b_router_expert"][lay], NE)).then_inc(S("router_in"), 16)
                if lay == 0:
                    pool.wait_ge(S("hn_ready"), 2 * NT)
                    pool.dma_start(gb[:, :], row(a["norm_mix"][1], D)).then_inc(S("gain_in"), 16)
                    pool.wait_ge(S("moe_done"), 1)
                    pool.dma_start(CC[0:120, 0, :], a["cache_conv"][0, 0:4].rearrange("b t c -> (b t) c")
                                   ).then_inc(S("conv_in"), 16)
                    pool.dma_start(CC[0:120, 1, :], a["cache_conv"][0, 4:8].rearrange("b t c -> (b t) c")
                                   ).then_inc(S("conv_in"), 16)
                    pool.dma_start(WDR[0:CONV_W, :], a["w_dw"][0]).then_inc(S("conv_in"), 16)
                    pool.dma_start(SMR[0:16, :], a["b_pw1"][0].rearrange("(c p) -> c p", p=P)
                                   ).then_inc(S("conv_in"), 16)
                    for i, name in enumerate(("b_dw", "conv_ln_g", "conv_ln_b")):
                        pool.dma_start(SMR[16 + 8 * i:24 + 8 * i, :], a[name][0].rearrange("(c p) -> c p", p=P)
                                       ).then_inc(S("conv_in"), 16)
                    pool.wait_ge(S("hn_ready"), 3 * NT)
                    pool.dma_start(gb[:, :], row(a["norm_ffn"][1], D)).then_inc(S("gain_in"), 16)
                    pool.wait_ge(S("ctok_ready"), 2)
                    store(o["conv_prompt"][0, 0], CP[0:HIST, :])
                    for b in range(NS):
                        store(o["conv_sample"][0, b, HIST - LS:HIST, :], CS[LS * b:LS * (b + 1), :])
                    pool.wait_ge(S("stored"), 16 * (STATE_STORES + CONV_STORES))
            pool.wait_ge(S("moe_done"), 2)
            for t in range(2):
                store(o["y_prompt"].rearrange("b (t p) d -> p (b t) d", p=P)[:, t, :], X[:, t, :])
            store(o["y_sample"].rearrange("b l d -> (b l) d"), X[:, 2, :])
            pool.wait_ge(S("stored"), 16 * (STATE_STORES + CONV_STORES + NT))
            pool.wait_ge(S("k_stored"), 32)
            pool.wait_ge(S("mix_stored"), 16 * 5)

        @block.tensor
        def _(pe):
            mm = nc.tensor.matmul
            full_seen = {}

            def full(seg, i):
                pe.wait_ge(S(f"{seg}_full{i % LO}"), 16 * (i // LO + 1))

            def transpose_stream(src):
                for k in range(KD):
                    for t in range(NT):
                        v = src[:, t, 0:D].rearrange("p (q k) -> p k q", k=KD)[:, k, :]
                        last = nc.tensor.transpose(PS[:, k, P * t:P * (t + 1)], v, ident)
                    last.then_inc(S("tr_done"), 1)

            def wait_stream(n):
                pe.wait_ge(S("tr_even"), 4 * n)
                pe.wait_ge(S("tr_odd"), 4 * n)

            pe.wait_ge(S("cst_in"), 16)
            pe.wait_ge(S("hn_ready"), NT)
            transpose_stream(HN)
            wait_stream(1)
            for u in range(N_IN):
                full("a", u)
                if u >= 4:
                    pe.wait_ge(S("pj_ready"), u - 3)
                b0 = 2 * (u % 4)
                w = dense(u)
                if u == FF_COL // UCOL - 1:
                    pe.wait_ge(S("mix_in"), 16 * MIX_LOADS)
                    for t in range(NT):
                        for k in range(KD):
                            mm(PS[:, b0 + 1, UCOL + FH * t:UCOL + FH * (t + 1)], HT[:, k, P * t:P * (t + 1)],
                               WF[:, k, :], start=k == 0, stop=k == KD - 1)
                for t in range(NT):
                    for k in range(KD):
                        last = mm(PS[:, b0 + t // 2, UCOL * (t % 2):UCOL * (t % 2) + UCOL],
                                  HT[:, k, P * t:P * (t + 1)], w[:, k, :], start=k == 0, stop=k == KD - 1)
                last.then_inc(S("proj_done"), 1)
            pe.wait_ge(S("pj_ready"), N_IN)
            pe.wait_ge(S("lf_ready"), 1)
            mm(PS[:, 0, 0:8], C["tri"], LF[:, 0, :], start=True, stop=True)
            mm(PS[:, 0, 8:16], C["tri"], LF[:, 1, :], start=True, stop=False)
            mm(PS[:, 0, 8:16], C["ones"], LF[:, 0, :], start=False, stop=True)
            mm(PS[:, 0, 16:24], C["blk"], LF[:, 2, :], start=True, stop=False)
            for b in range(NS):
                one = C["sel"][:, P - LS - LS * b:2 * P - LS - LS * b]
                mm(PS[:, 0, 16:24], one, CLF[:, b, :], start=False, stop=b == NS - 1)
            mm(PS[0:FH, 1, 0:P], LF[:, 0, :], C["tri"], start=True, stop=True)
            mm(PS[0:FH, 1, P:2 * P], LF[:, 1, :], C["tri"], start=True, stop=False)
            mm(PS[0:FH, 1, P:2 * P], LF[:, 0, :], C["ones"], start=False, stop=True)
            for b in range(NS):
                out = PS[0:FH, 2 + b // 3, KEYS * (b % 3):KEYS * (b % 3) + KEYS]
                mm(out[:, 0:PAST], CLF[:, b, :], C["tri"], start=True, stop=True)
                mm(out[:, PAST:KEYS], CLF[:, b, :], C["ones"][:, 0:LS], start=True, stop=False)
                last = mm(out[:, PAST:KEYS], LF[:, 2, :], C["blk"][:, LS * b:LS * (b + 1)], start=False, stop=True)
            last.then_inc(S("csum_done"), 1)
            pe.wait_ge(S("q_ready"), 1)
            pe.wait_ge(S("k_ready"), 1)
            pe.wait_ge(S("csum_read"), 4)
            for i in range(2 * FH):
                h, isk = divmod(i, 2)
                if i >= 8:
                    pe.wait_ge(S("kt_ready" if isk else "qt_ready"), h - 3)
                for t in range(NT):
                    c0 = (KO if isk else QO) + FD * h
                    last = nc.tensor.transpose(PS[0:FD, i % 8, P * t:P * (t + 1)], PJ[:, t, c0:c0 + FD], ident)
                last.then_inc(S("qk_tr"), 1)
            pe.wait_ge(S("qt_ready"), FH)
            pe.wait_ge(S("kt_ready"), FH)

            def scores(h):
                if h >= 2:
                    pe.wait_ge(S("scores_masked"), h - 1)
                mm(PS[:, h % 2, 0:P], QT[0:72, h, 0:P], KT[0:72, h, 0:P], start=True, stop=True)
                mm(PS[:, h % 2, P:3 * P], QT[0:72, h, P:2 * P], KT[0:72, h, 0:2 * P], start=True, stop=True
                   ).then_inc(S("scores_done"), 1)

            scores(0)
            for h in range(FH + 1):
                if h + 1 < FH:
                    scores(h + 1)
                if h < FH:
                    pe.wait_ge(S("probs_ready"), h + 1)
                    if h >= 2:
                        pe.wait_ge(S("probsT_ready"), h - 1)
                    for i in range(3):
                        last = nc.tensor.transpose(PS[:, 2 + h % 2, P * i:P * (i + 1)],
                                                   SS[:, h % 2, P * i:P * (i + 1)], ident)
                    last.then_inc(S("probs_tr"), 1)
                if h >= 1:
                    g = h - 1
                    pe.wait_ge(S("probsT_ready"), g + 1)
                    if g >= 2:
                        pe.wait_ge(S("attn_out"), g - 1)
                    v = [PJ[:, t, VO + FD * g:VO + FD * (g + 1)] for t in range(2)]
                    mm(PS[:, 4 + g % 2, 0:FD], PT[:, g % 2, 0:P], v[0], start=True, stop=True)
                    mm(PS[:, 4 + g % 2, FD:2 * FD], PT[:, g % 2, P:2 * P], v[0], start=True, stop=False)
                    mm(PS[:, 4 + g % 2, FD:2 * FD], PT[:, g % 2, 2 * P:3 * P], v[1], start=False, stop=True
                       ).then_inc(S("attn_done"), 1)
            pe.wait_ge(S("attn_out"), FH)
            for b in range(NS):
                n = N_IN + b // 4
                if b % 4 == 0:
                    full("a", n)
                if b >= 2:
                    pe.wait_ge(S("ktc_even" if b % 2 == 0 else "ktc_odd"), b // 2)
                kc = slot[n % LO][:, :].rearrange("p (b c) -> p b c", b=4)
                for h in range(FH):
                    last = nc.tensor.transpose(PS[0:FD, 2 * (b % 2) + h // 4, P * (h % 4):P * (h % 4) + P],
                                               kc[:, b % 4, FD * h:FD * (h + 1)], ident)
                last.then_inc(S("cachek_tr"), 1)
            pe.wait_ge(S("ktc_even"), 4)
            pe.wait_ge(S("ktc_odd"), 4)
            pe.wait_ge(S("ktc_new"), 1)
            for h in range(FH):
                if h >= 4:
                    pe.wait_ge(S("s_masked"), h - 3)
                for par in range(2):
                    for j in range(4):
                        last = mm(PS[32 * j:32 * j + 32, 4 + h % 4, KEYS * par:KEYS * (par + 1)],
                                  QT[0:72, h, 2 * P + 32 * j:2 * P + 32 * j + 32], KTC[0:72, 2 * j + par, h, :],
                                  start=True, stop=True, tile_position=(0, 32 * j))
                last.then_inc(S("s_done"), 1)
            pe.wait_ge(S("s_probs"), 1)
            full("a", N_IN + 2)
            full("a", N_IN + 3)

            def sample_out(h):
                pe.wait_ge(S("sT_ready"), h + 1)
                out = PS[:, 6, FD * h:FD * (h + 1)]
                mm(out, PT[:, h % 2, 2 * P:3 * P], PJ[:, 2, VO + FD * h:VO + FD * (h + 1)], start=True, stop=False,
                   skip_group_check=True)
                for par in range(2):
                    for j in range(4):
                        b = 2 * j + par
                        vc = slot[(N_IN + 2 + b // 4) % LO][:, :].rearrange("p (b c) -> p b c", b=4)
                        last = mm(out[32 * j:32 * j + 32, :], PT[:, h % 2, P * par + 32 * j:P * par + 32 * j + 32],
                                  vc[:, b % 4, FD * h:FD * (h + 1)], start=False, stop=par == 1,
                                  skip_group_check=True, tile_position=(0, 32 * j))
                last.then_inc(S("so_done"), 1)

            for h in range(FH + 1):
                if h < FH:
                    if h >= 2:
                        pe.wait_ge(S("sT_ready"), h - 1)
                        pe.wait_ge(S("so_done"), h - 1)
                    for i in range(3):
                        src = PN[:, h, :] if i == 2 else ES[:, 2 * h + i, 0:PAST]
                        last = nc.tensor.transpose(PS[:, h % 2, P * i:P * (i + 1)], src, ident)
                    last.then_inc(S("sT_done"), 1)
                if h >= 1:
                    sample_out(h - 1)
            last = nc.tensor.transpose(PS[:, 7, 0:P], ident, ident)
            last.then_inc(S("cachev_used"), 1)

            pe.wait_ge(S("rot_ready"), 1)
            pe.wait_ge(S("fox_done"), 1)
            for i in range(2 * RH):
                for t in range(NT):
                    last = nc.tensor.transpose(PS[0:RK, i, P * t:P * (t + 1)], RT[:, t, i, :], ident)
                last.then_inc(S("ret_tr"), 1)
            pe.wait_ge(S("qrt_even"), 4)
            pe.wait_ge(S("qrt_odd"), 4)
            pe.wait_ge(S("qd_ready"), 1)

            def ret_scores(h):
                if h >= 2:
                    pe.wait_ge(S("sd_ready"), h - 1)
                for t in range(NT):
                    tt = slice(P * t, P * (t + 1))
                    last = mm(PS[:, h % 2, tt], QRT[0:RK, RH + h, tt], QRT[0:RK, h, tt], start=True, stop=True)
                last.then_inc(S("rs_done"), 1)
                if h >= 2:
                    pe.wait_ge(S("s2_ready"), h - 1)
                for t in range(2):
                    last = mm(PS[0:RK, 4 + h % 2, P * t:P * (t + 1)], KDP[:, t, h, :],
                              PJ[:, t, RVO + RV * h:RVO + RV * (h + 1)], start=True, stop=True)
                last.then_inc(S("sadd_done"), 1)

            ret_scores(0)
            for h in range(RH):
                if h + 1 < RH:
                    ret_scores(h + 1)
                pe.wait_ge(S("sd_ready"), h + 1)
                pe.wait_ge(S("s2_ready"), h + 1)
                if h >= 2:
                    pe.wait_ge(S("yr_ready"), h - 1)
                v = [PJ[:, t, RVO + RV * h:RVO + RV * (h + 1)] for t in range(NT)]
                mm(PS[:, 2 + h % 2, 0:P], SD[:, h % 2, 0:P], v[0], start=True, stop=True)
                mm(PS[:, 2 + h % 2, P:2 * P], SD[:, h % 2, P:2 * P], v[1], start=True, stop=False)
                mm(PS[:, 2 + h % 2, P:2 * P], QD1[0:RK, h, :], S1[0:RK, h, 0, :], start=False, stop=True)
                out = PS[:, 2 + h % 2, 2 * P:3 * P]
                mm(out, SD[:, h % 2, 2 * P:3 * P], v[2], start=True, stop=False, skip_group_check=True)
                for j in range(4):
                    last = mm(out[32 * j:32 * j + 32, :], QD2[:, h, 32 * j:32 * j + 32], STt[:, j, h, :],
                              start=False, stop=True, skip_group_check=True, tile_position=(0, 32 * j))
                last.then_inc(S("y_done"), 1)
            pe.wait_ge(S("vm_ready"), 1)
            for j in range(4):
                if j >= 2:
                    pe.wait_ge(S("stn_ready"), j - 1)
                for h in range(RH):
                    last = mm(PS[:, 6 + j % 2, RV * h:RV * (h + 1)], KDS[:, h, :, :],
                              VM[:, j, RV * h:RV * (h + 1)], start=True, stop=True)
                last.then_inc(S("sstate_done"), 1)

            pe.wait_ge(S("mix_ready"), 1)
            transpose_stream(PJ)
            wait_stream(2)

            def project_out(seg, first, lhs, done, added):
                for u in range(4):
                    full(seg, first + u)
                    if u >= 2:
                        pe.wait_ge(S("x_mixed"), added + 2 * (u - 1))
                    w = dense(first + u)
                    for t in range(NT):
                        for k in range(KD):
                            last = mm(PS[:, 2 * (u % 2) + t // 2, UCOL * (t % 2):UCOL * (t % 2) + UCOL],
                                      lhs[:, k, P * t:P * (t + 1)], w[:, k, :], start=k == 0, stop=k == KD - 1)
                    last.then_inc(S(done), 1)

            project_out("a", N_IN + 4, HT, "wout_done", 0)

            def moe(lay, stream, base):
                pe.wait_ge(S("hn_ready"), NT * (2 * lay + 2))
                transpose_stream(NM)
                wait_stream(stream)
                pe.wait_ge(S("router_in"), 64 * (lay + 1))
                for t in range(NT):
                    for k in range(KD):
                        last = mm(PS[:, 0, NR * t:NR * (t + 1)], HM[:, k, P * t:P * (t + 1)], WR[:, k, :],
                                  start=k == 0, stop=k == KD - 1)
                last.then_inc(S("logits_done"), 1)
                pe.wait_ge(S("chosen"), lay + 1)
                for t in range(NT):
                    out = PS[:, 1, NE * t:NE * (t + 1)]
                    for s in range(t):
                        mm(out, C["ones"], SE[:, s, :], start=s == 0, stop=False)
                    mm(out, C["strict"], SE[:, t, :], start=t == 0, stop=True)
                for t in range(NT):
                    last = mm(PS[:, 1, NE * NT:NE * (NT + 1)], C["ones"], SE[:, t, :], start=t == 0, stop=t == NT - 1)
                last.then_inc(S("ranks_done"), 1)

                def gather(half):
                    for kk in range(4):
                        k = 4 * half + kk
                        out = PS[:, kk // 2, 256 * (kk % 2):256 * (kk % 2) + 256]
                        for t in range(NT):
                            for part, x in enumerate((XHI, XLO)):
                                v = x[:, t, :].rearrange("p (q k) -> p k q", k=KD)[:, k, :]
                                last = mm(out, v, G[:, QUAD * t:QUAD * (t + 1), :], start=t + part == 0,
                                          stop=t + part == NT)
                    last.then_inc(S("gathered"), 1)

                def gate_up(pair):
                    for e in range(2):
                        for gu in range(2):
                            w = slot[6 * pair + 2 * e + gu][:, :].rearrange("p (k f) -> p k f", k=KD)
                            for ft in range(2):
                                c0 = CAP * (4 * gu + 2 * e + ft)
                                for k in range(KD):
                                    last = mm(PS[:, 2 + pair, c0:c0 + CAP], w[:, k, P * ft:P * (ft + 1)],
                                              XG[:, k, CAP * (2 * pair + e):CAP * (2 * pair + e + 1)],
                                              start=k == 0, stop=k == KD - 1)
                        last.then_inc(S("gu_done"), 1)

                def down(pair, s):
                    for e in range(2):
                        pe.wait_ge(S(f"d_full{2 * pair + e}"), (s + 1) * 16)
                        w = slot[6 * pair + 4 + e][:, :].rearrange("p (j n) -> p j n", j=2)
                        for n in range(2):
                            for j in range(2):
                                last = mm(PS[CAP * e:CAP * (e + 1), 4 + n, :], HID[:, pair, e, j, :],
                                          w[:, j, 512 * n:512 * (n + 1)], start=j == 0, stop=j == 1)
                        last.then_inc(S("d_done"), 1)

                def step(s, more):
                    pe.wait_ge(S("xg_ready"), (s + 1) * 2)
                    pe.wait_ge(S("hid_ready"), s * 2 + 1)
                    for e in range(2):
                        pe.wait_ge(S(f"gu_full{e}"), (s + 1) * 32)
                    gate_up(0)
                    pe.wait_ge(S("gw_ready"), s + 1)
                    pe.wait_ge(S("x_added"), s * 6 + 6)
                    for pair in range(2):
                        for t in range(NT):
                            last = nc.tensor.transpose(PS[:, 6 + pair, P * t:P * (t + 1)],
                                                       GW[:, QUAD * t + 2 * pair:QUAD * t + 2 * pair + 2, :], ident)
                        last.then_inc(S("gw_tr"), 1)
                    pe.wait_ge(S("hid_ready"), s * 2 + 2)
                    for e in range(2, 4):
                        pe.wait_ge(S(f"gu_full{e}"), (s + 1) * 32)
                    gate_up(1)
                    pe.wait_ge(S("hid_ready"), s * 2 + 3)
                    pe.wait_ge(S("yl_ready"), s * 2 + 2)
                    down(0, s)
                    if more:
                        pe.wait_ge(S("g_ready"), s + 2)
                        gather(0)
                    pe.wait_ge(S("hid_ready"), s * 2 + 4)
                    pe.wait_ge(S("yl_ready"), s * 2 + 3)
                    down(1, s)
                    if more:
                        pe.wait_ge(S("xg_ready"), s * 2 + 3)
                        gather(1)
                    pe.wait_ge(S("gt_ready"), s * 4 + 4)
                    pe.wait_ge(S("yl_ready"), s * 2 + 4)
                    for i in range(2 * NT):
                        t, n = divmod(i, 2)
                        pe.wait_ge(S("x_added"), s * 6 + i + 5)
                        for pair in range(2):
                            for part, y in enumerate((YH, YL)):
                                last = mm(PS[:, 6 + i % 2, :], GT[:, pair, P * t:P * (t + 1)],
                                          y[:, pair, 512 * n:512 * (n + 1)], start=pair + part == 0,
                                          stop=pair + part == 2)
                        last.then_inc(S("sum_done"), 1)

                pe.wait_ge(S("steps_known"), lay + 1)
                n = pe.value_load(NW[0:1, lay:lay + 1], min_val=0, max_val=(MAXWIN - 1) * NQ) + NQ
                pe.wait_ge(S("g_ready"), base + 1)
                gather(0)
                pe.wait_ge(S("xg_ready"), base * 2 + 1)
                gather(1)
                with pe.Fori(base, base + n - 1) as s:
                    step(s, True)
                step(base + n - 1, False)
                return n

            steps0 = moe(0, 3, 0)

            pe.wait_ge(S("conv_in"), 16 * 7)
            pe.wait_ge(S("moe_done"), 1)
            nc.tensor.transpose(PS[:, 6, 0:40], SMR[0:40, :], ident[0:40, 0:40])
            for c in range(KD):
                last = nc.tensor.transpose(PS[:, 6, 64 + 32 * c:64 + 32 * c + CONV_W], WDR[0:CONV_W, P * c:P * (c + 1)],
                                           ident[0:CONV_W, 0:CONV_W])
            last.then_inc(S("taps_tr"), 1)
            for c in range(KD):
                bank = 2 * (c % 2) + (c // 2) % 2
                if c >= 4:
                    pe.wait_ge(S("hist_ready"), c - 3)
                for g in range(2):
                    last = nc.tensor.transpose(PS[:, bank, 120 * g:120 * (g + 1)], CC[0:120, g, P * c:P * (c + 1)],
                                               ident[0:120, 0:120])
                last.then_inc(S("hist_tr"), 1)
            pe.wait_ge(S("hist_ready"), KD)
            pe.wait_ge(S("taps_ready"), 2)
            pe.wait_ge(S("hn_ready"), 3 * NT)
            transpose_stream(NC)
            wait_stream(4)
            for c in range(KD):
                m, cc = divmod(c, 2)
                if cc == 0:
                    full("c", 2 * m)
                    full("c", 2 * m + 1)
                if c >= 2:
                    pe.wait_ge(S("u_ready"), c - 1)
                for g in range(2):
                    w = dense(2 * m + g)
                    for k in range(KD):
                        last = mm(PS[:, 2 * (c % 2) + g, 0:TOK], w[:, k, P * cc:P * (cc + 1)], HC[:, k, :],
                                  start=k == 0, stop=k == KD - 1)
                    if g == 0 and cc == 1:
                        last.then_inc(S("pw_done"), 1)
                    if g == 1:
                        last.then_inc(S("glu_done"), 1)
                        if cc == 1:
                            nc.tensor.transpose(PS[0:32, 7, 0:32], ident[0:32, 0:32], ident[0:32, 0:32]
                                                ).then_inc(S("pw_done"), 1)
            pe.wait_ge(S("unew_ready"), KD)
            for c in range(KD):
                nc.tensor.transpose(PS[0:HIST, c // 4, P * (c % 4):P * (c % 4 + 1)], U[:, c, SEQ:SEQ + HIST], ident)
                last = nc.tensor.transpose(PS[:, 2 + c // 4, P * (c % 4):P * (c % 4 + 1)], YS[:, c, 0:P], ident)
            last.then_inc(S("ctok_tr"), 1)
            for c in range(KD):
                pe.wait_ge(S("y_conv"), c + 1)
                last = mm(PS[:, 6, 0:TOK], C["onesd"], YC[:, c, :], start=c == 0, stop=c == KD - 1)
            last.then_inc(S("mean_done"), 1)
            pe.wait_ge(S("ysq_ready"), 1)
            for c in range(KD):
                last = mm(PS[:, 7, 0:TOK], C["onesd"], YS[:, c, :], start=c == 0, stop=c == KD - 1)
            last.then_inc(S("var_done"), 1)
            pe.wait_ge(S("z_ready"), KD)
            pe.wait_ge(S("ctok_ready"), 2)
            project_out("c", 8, YC, "pw_done", 8)

            moe(1, 5, steps0)

        @block.scalar
        def _(act):
            q = InOrder(act, S("act_step"))
            A = nc.scalar.activation
            ev = [0]

            def norm_stats(n, dst):
                for t in range(NT):
                    q.do(A(dst[:, t, :], X[:, t, :], ACT.Square, accum_out=stat[:, t:t + 1]))
                q.settle()
                q.link(A(stat[:, 3:6], stat[:, 0:3], ACT.Sqrt, scale=1.0 / D, bias=C["eps"]), S("rms_ready"))

            def stream_even(n, dst):
                for k in range(0, KD, 2):
                    act.wait_ge(S("tr_done"), KD * n + k + 1)
                    q.do(A(dst[:, k, :], PS[:, k, 0:TOK], ACT.Copy), S("tr_even"))

            act.wait_ge(S("x_in"), 16 * (NT + 1))
            act.wait_ge(S("cst_in"), 16)
            norm_stats(0, HN)
            stream_even(0, HT)
            for u in range(N_IN):
                act.wait_ge(S("proj_done"), u + 1)
                b0 = 2 * (u % 4)
                q.do(A(PJ[:, 0:2, UCOL * u:UCOL * (u + 1)], PS[:, b0, :].rearrange("p (t n) -> p t n", t=2), ACT.Copy))
                if u == FF_COL // UCOL - 1:
                    q.do(A(FF[:, :, :], PS[:, b0 + 1, UCOL:UCOL + NT * FH].rearrange("p (t n) -> p t n", t=NT),
                           ACT.Copy))
                q.do(A(PJ[:, 2, UCOL * u:UCOL * (u + 1)], PS[:, b0 + 1, 0:UCOL], ACT.Copy), S("pj_ready"))
                if u == 3:
                    act.wait_ge(S("qk_sumsq"), 1)
                    q.link(A(MS[:, :], MS[:, :], ACT.Sqrt, scale=1.0 / FD, bias=C["eps"]), S("qk_rms"))
                if u == 5:
                    act.wait_ge(S("qk_sumsq"), 2)
                    q.link(A(MS[:, :], MS[:, :], ACT.Sqrt, scale=1.0 / FD, bias=C["eps"]), S("qk_rms"))
            act.wait_ge(S("ff_abs"), 1)
            q.link(A(LT[:, :, :], LT[:, :, :], ACT.Exp, scale=-1.0))
            q.link(A(LT[:, :, :], LT[:, :, :], ACT.Ln, bias=1.0), S("ff_ln"))
            act.wait_ge(S("csum_done"), 1)
            q.do(A(CQ[:, :, :], PS[:, 0, 0:NT * FH].rearrange("p (t h) -> p t h", t=NT), ACT.Copy))
            q.do(A(KT[FD:FD + FH, :, 0:SEQ], bc(PS[0:FH, 1, 0:SEQ], 1, FH), ACT.Copy, scale=-1.0))
            for g in range(3):
                nb = 3 if g < 2 else 2
                for b in range(3 * g, 3 * g + nb):
                    ins = A(KTC[FD:FD + FH, b, :, :], bc(PS[0:FH, 2 + g, KEYS * (b % 3):KEYS * (b % 3 + 1)], 1, FH),
                            ACT.Copy, scale=-1.0)
                    q.do(ins, S("csum_read") if b in (2, 5, 6, 7) else None)
            for h in range(FH):
                act.wait_ge(S("qk_tr"), 2 * h + 1)
                q.do(A(QT[0:FD, h, :], PS[0:FD, (2 * h) % 8, 0:TOK], ACT.Copy), S("qt_ready"))
            def exps(h):
                act.wait_ge(S("scores_masked"), h + 1)
                q.do(A(SS[:, h % 2, 0:P], SS[:, h % 2, 0:P], ACT.Exp, bias=MX[:, 2 * (h % 2):2 * (h % 2) + 1],
                       accum_out=SM[:, 2 * (h % 2):2 * (h % 2) + 1]))
                q.do(A(SS[:, h % 2, P:3 * P], SS[:, h % 2, P:3 * P], ACT.Exp,
                       bias=MX[:, 2 * (h % 2) + 1:2 * (h % 2) + 2],
                       accum_out=SM[:, 2 * (h % 2) + 1:2 * (h % 2) + 2]), S("probs_ready"))

            exps(0)
            for h in range(FH):
                if h + 1 < FH:
                    if h >= 1:
                        act.wait_ge(S("attn_out"), h)
                    exps(h + 1)
                act.wait_ge(S("probs_tr"), h + 1)
                if h >= 2:
                    act.wait_ge(S("attn_done"), h - 1)
                q.do(A(PT[:, h % 2, :], PS[:, 2 + h % 2, 0:TOK], ACT.Copy), S("probsT_ready"))
            for b in range(0, NS, 2):
                act.wait_ge(S("cachek_tr"), b + 1)
                q.do(A(KTC[0:FD, b, :, 0:PAST], PS[0:FD, 0:2, :].rearrange("p a (h n) -> p (a h) n", n=PAST),
                       ACT.Copy), S("ktc_even"))
            act.wait_ge(S("s_centred"), 1)
            q.do(A(ES[:, :, :], ES[:, :, :], ACT.Exp), S("s_exp"))
            for h in range(0, FH, 2):
                act.wait_ge(S("sT_done"), h + 1)
                if h >= 2:
                    act.wait_ge(S("so_done"), h - 1)
                q.do(A(PT[:, 0, :], PS[:, 0, 0:TOK], ACT.Copy), S("sT_even"))
            act.wait_ge(S("fox_done"), 1)
            act.wait_ge(S("vm_zero"), 1)
            for j in range(4):
                q.do(A(VM[32 * j:32 * j + 32, j, :], PJ[32 * j:32 * j + 32, 2, RVO:RGO], ACT.Copy),
                     S("vm_ready") if j == 3 else None)
            q.do(A(PJ[:, :, RGO:MIX], PJ[:, :, RGO:MIX], ACT.Silu), S("rg_silu"))
            for i in range(0, 2 * RH, 2):
                act.wait_ge(S("ret_tr"), i + 1)
                q.do(A(QRT[0:RK, i, :], PS[0:RK, i, 0:TOK], ACT.Copy), S("qrt_even"))
            act.wait_ge(S("qrt_odd"), 2)
            q.settle()
            q.do(A(QD2[0:RK, :, :], QRT[0:RK, 0:RH, SEQ:TOK], ACT.Copy))
            q.do(A(QD2[RK:P, :, :], QRT[0:RK, 0:RH, SEQ:TOK], ACT.Copy), S("qd2_in"))
            for h in range(RH):
                act.wait_ge(S("y_done"), h + 1)
                q.do(A(YR[:, :, h, :], PS[:, 2 + h % 2, 0:TOK].rearrange("p (t v) -> p t v", t=NT), ACT.Copy),
                     S("yr_ready"))
            act.wait_ge(S("yr_centred"), 1)
            q.link(A(YQ[:, :, :, :], YR[:, :, :, :], ACT.Square), S("yr_sq"))
            act.wait_ge(S("yr_sumsq"), 1)
            q.link(A(stat[:, 0:12], stat[:, 0:12], ACT.Sqrt, scale=1.0 / RV, bias=C["eps"]), S("yr_rms"))
            stream_even(1, HT)

            def moe(lay, stream, base):
                act.wait_ge(S("x_mixed"), 8 * (lay + 1))
                act.wait_ge(S("stored"), 16 * (STATE_STORES + lay * CONV_STORES))
                norm_stats(2 * lay + 1, NM)
                stream_even(stream - 1, HM)
                act.wait_ge(S("gl_centred"), lay + 1)
                q.link(A(E4[:, :, :], E4[:, :, :], ACT.Exp), S("gl_exp"))
                act.wait_ge(S("d_ready"), lay + 1)
                q.link(A(R8[:, 21:24], R8[:, 18:21], ACT.Exp), S("d_exp"))

                def xg(half):
                    q2 = A(XG[:, 4 * half:4 * half + 4, :].rearrange("p k n -> p (k n)"),
                           PS[:, 0:2, :].rearrange("p a n -> p (a n)"), ACT.Copy)
                    q2.then_inc(S("xg_ready"), 1)

                def step(s, more):
                    for pair in range(2):
                        act.wait_ge(S("gu_done"), s * 4 + (2 * pair + 2))
                        A(SG[:, pair, :, :].rearrange("p e n -> p (e n)"), PS[:, 2 + pair, 0:4 * CAP],
                          ACT.Silu).then_inc(S("silu_ready"), 1)
                    for pair in range(2):
                        act.wait_ge(S("d_done"), s * 4 + (2 * pair + 2))
                        act.wait_ge(S("gt_ready"), s * 4 + (2 * pair + 2))
                        A(YH[:, pair, :], PS[:, 4:6, :].rearrange("p a n -> p (a n)"), ACT.Copy,
                          scale=GATE[:, pair:pair + 1]).then_inc(S("yh_ready"), 1)
                        if more:
                            act.wait_ge(S("gathered"), s * 2 + (3 + pair))
                            xg(pair)

                act.wait_ge(S("steps_known"), lay + 1)
                n = act.value_load(NW[0:1, lay:lay + 1], min_val=0, max_val=(MAXWIN - 1) * NQ) + NQ
                for half in range(2):
                    act.wait_ge(S("gathered"), base * 2 + (half + 1))
                    xg(half)
                with act.Fori(base, base + n - 1) as s:
                    step(s, True)
                step(base + n - 1, False)
                return n

            steps0 = moe(0, 3, 0)
            act.wait_ge(S("moe_done"), 1)
            norm_stats(2, NC)
            act.wait_ge(S("taps_tr"), 1)
            q.do(A(SMT[:, :], PS[:, 6, 0:40], ACT.Copy), S("taps_ready"))
            q.do(A(WDT[:, :, :], PS[:, 6, 64:64 + 32 * KD].rearrange("p (c w) -> p c w", c=KD)[:, :, 0:CONV_W],
                   ACT.Copy), S("taps_ready"))
            for c in range(KD):
                act.wait_ge(S("hist_tr"), c + 1)
                v = U[:, c, HIST + SEQ:WID].rearrange("p (b w) -> p b w", b=NS)[:, :, 0:HIST]
                q.do(A(v, PS[:, 2 * (c % 2) + (c // 2) % 2, 0:240].rearrange("p (b w) -> p b w", b=NS), ACT.Copy),
                     S("hist_ready"))
            stream_even(3, HC)
            q.settle()
            for c in range(KD):
                act.wait_ge(S("glu_done"), c + 1)
                if c >= 2:
                    act.wait_ge(S("u_ready"), c - 1)
                q.do(A(SGC[:, c % 2, :], PS[:, 2 * (c % 2) + 1, 0:TOK], ACT.Sigmoid, bias=SMT[:, 8 + c:9 + c]),
                     S("sig_ready"))
                act.wait_ge(S("u_ready"), c + 1)
                v = U[:, c, HIST + SEQ:WID].rearrange("p (b w) -> p b w", b=NS)[:, :, HIST:]
                q.do(A(YS[:, c, 0:P].rearrange("p (b l) -> p b l", b=NS), v, ACT.Copy), S("unew_ready"))
            act.wait_ge(S("ctok_tr"), 1)
            q.do(A(CP[0:HIST, :], PS[0:HIST, 0:2, :].rearrange("p a n -> p (a n)"), ACT.Copy), S("ctok_ready"))
            q.do(A(CS[:, :], PS[:, 2:4, :].rearrange("p a n -> p (a n)"), ACT.Copy), S("ctok_ready"))
            act.wait_ge(S("yc_centred"), 1)
            q.do(A(YS[:, :, :], YC[:, :, :], ACT.Square), S("ysq_ready"))
            act.wait_ge(S("var_done"), 1)
            q.link(A(VR[:, :], PS[:, 7, 0:TOK], ACT.Sqrt, bias=C["eps"]), S("cstd_ready"))
            act.wait_ge(S("yc_normed"), 1)
            for c in range(KD):
                q.do(A(YC[:, c, :], YC[:, c, :], ACT.Silu, scale=SMT[:, 24 + c:25 + c], bias=SMT[:, 32 + c:33 + c]),
                     S("z_ready"))
            moe(1, 5, steps0)

        @block.vector
        def _(dve):
            q = InOrder(dve, S("dve_step"))
            V = nc.vector

            def tt(out, in0, in1, op, sem=None):
                q.link(V.tensor_tensor(out, in0, in1, op), sem)

            def ts(out, in0, s1, s2, op0, op1=None, sem=None):
                if op1 is None:
                    q.link(V.tensor_scalar(out, in0, s1, None, op0), sem)
                else:
                    q.link(V.tensor_scalar(out, in0, s1, s2, op0, op1), sem)

            def red(out, in_, op, sem=None, negate=None):
                q.link(V.tensor_reduce(out=out, in_=in_, axis=AXX, op=op, negate=negate), sem)

            def norm_apply(n, dst):
                dve.wait_ge(S("rms_ready"), n + 1)
                if n:
                    dve.wait_ge(S("gain_in"), 16 * n)
                else:
                    dve.wait_ge(S("x_in"), 16 * (NT + 1))
                q.link(V.reciprocal(stat[:, 6:9], stat[:, 3:6]))
                for t in range(NT):
                    q.do(V.scalar_tensor_tensor(dst[:, t, :], X[:, t, :], stat[:, 6 + t:7 + t], gb[:, :], ALU.mult,
                                                ALU.mult), S("hn_ready"))
                q.settle()

            def stream_odd(n, dst):
                for k in range(1, KD, 2):
                    dve.wait_ge(S("tr_done"), KD * n + k + 1)
                    q.do(V.tensor_copy(dst[:, k, :], PS[:, k, 0:TOK]), S("tr_odd"))
                q.settle()

            norm_apply(0, HN)
            stream_odd(0, HT)
            for i, (c0, gain) in enumerate(((QO, GQ), (KO, GK))):
                dve.wait_ge(S("pj_ready"), 2 * i + 2)
                if i == 0:
                    dve.wait_ge(S("mix_in"), 16 * MIX_LOADS)
                    ts(GQ[:, :], GQ[:, :], FD ** -0.5, None, ALU.mult)
                src = PJ[:, :, c0:c0 + FH * FD]
                tt(SQ[:, :, :], src, src, ALU.mult)
                red(MS[:, :].rearrange("p (t h) -> p t h", t=NT), SQ[:, :, :].rearrange("p t (h d) -> p t h d", d=FD),
                    ALU.add, S("qk_sumsq"))
                dve.wait_ge(S("qk_rms"), i + 1)
                q.link(V.reciprocal(MS[:, :], MS[:, :]))
                for t in range(NT):
                    v = PJ[:, t, c0:c0 + FH * FD].rearrange("p (h d) -> p h d", d=FD)
                    tt(v, v, bc(MS[:, FH * t:FH * (t + 1)], 2, FD), ALU.mult)
                    tt(v, v, bc(gain[:, :], 1, FH), ALU.mult, S("q_ready" if i == 0 else "k_ready") if t == 2 else None)
            dve.wait_ge(S("pj_ready"), 6)
            tt(FF[:, :, :], FF[:, :, :], bc(BF[:, :], 1, NT), ALU.add)
            lt, ff = (v[:, :, :].rearrange("p t h -> p (t h)") for v in (LT, FF))
            q.link(V.scalar_tensor_tensor(lt, ff, -1.0, ff, ALU.mult, ALU.max), S("ff_abs"))
            ts(FF[:, :, :], FF[:, :, :], 0.0, None, ALU.min)
            dve.wait_ge(S("ff_ln"), 1)
            tt(LF[:, :, :], FF[:, :, :], LT[:, :, :], ALU.subtract, S("lf_ready"))
            for h in range(FH):
                dve.wait_ge(S("qk_tr"), 2 * h + 2)
                q.do(V.tensor_copy(KT[0:FD, h, :], PS[0:FD, (2 * h + 1) % 8, 0:TOK]), S("kt_ready"))
            q.settle()

            def mask(h):
                dve.wait_ge(S("scores_done"), h + 1)
                if h >= 2:
                    dve.wait_ge(S("probs_tr"), h - 1)
                m = 2 * (h % 2)
                q.do(V.scalar_tensor_tensor(SS[:, h % 2, 0:P], PS[:, h % 2, 0:P], CQ[:, 0, h:h + 1],
                                            C["mask"][:, P:2 * P], ALU.add, ALU.add))
                q.link(V.scalar_tensor_tensor(SS[:, h % 2, P:3 * P], PS[:, h % 2, P:3 * P], CQ[:, 1, h:h + 1],
                                              C["mask"], ALU.add, ALU.add))
                q.do(V.tensor_reduce(out=MX[:, m:m + 1], in_=SS[:, h % 2, 0:P], axis=AXX, op=ALU.max, negate=True))
                q.link(V.tensor_reduce(out=MX[:, m + 1:m + 2], in_=SS[:, h % 2, P:3 * P], axis=AXX, op=ALU.max,
                                       negate=True), S("scores_masked"))

            dve.wait_ge(S("csum_read"), 4)
            mask(0)
            for h in range(FH + 1):
                if h + 1 < FH:
                    mask(h + 1)
                if h >= 1:
                    g = h - 1
                    dve.wait_ge(S("attn_done"), g + 1)
                    m = 2 * (g % 2)
                    q.link(V.reciprocal(RR[:, m:m + 2], SM[:, m:m + 2]))
                    for t in range(2):
                        q.do(V.tensor_scalar(PJ[:, t, QO + FD * g:QO + FD * (g + 1)], PS[:, 4 + g % 2, FD * t:FD * (t + 1)],
                                             RR[:, m + t:m + t + 1], None, ALU.mult),
                             S("attn_out") if t else None)
                    q.settle()
            q.do(V.tensor_copy(KTC[0:FD, :, :, PAST:KEYS],
                               KT[0:FD, :, SEQ:TOK].rearrange("p h (b l) -> p b h l", l=LS)), S("ktc_new"))
            for b in range(1, NS, 2):
                dve.wait_ge(S("cachek_tr"), b + 1)
                q.do(V.tensor_copy(KTC[0:FD, b, :, 0:PAST], PS[0:FD, 2:4, :].rearrange("p a (h n) -> p (a h) n", n=PAST)),
                     S("ktc_odd"))
            q.settle()
            for h in range(FH):
                dve.wait_ge(S("s_done"), h + 1)
                q.do(V.scalar_tensor_tensor(ES[:, 2 * h:2 * h + 2, :],
                                            PS[:, 4 + h % 4, 0:2 * KEYS].rearrange("p (a n) -> p a n", a=2),
                                            CQ[:, 2, h:h + 1], bc(C["smask"], 1, 2), ALU.add, ALU.add), S("s_masked"))
            q.settle()
            red(MX[:, 0:16], ES[:, :, :], ALU.max)
            tt(ES[:, :, :], ES[:, :, :], bc(MX[:, 0:16], 2, KEYS), ALU.subtract, S("s_centred"))
            dve.wait_ge(S("s_done"), FH)
            q.link(V.memset(PN[:, :, :], 0.0))
            dve.wait_ge(S("s_exp"), 1)
            red(SM[:, 0:16], ES[:, :, :], ALU.add)
            q.link(V.reciprocal(RR[:, 0:16], SM[:, 0:16]))
            tt(RR[:, 0:16].rearrange("p (h a) -> p h a", a=2), RR[:, 0:16].rearrange("p (h a) -> p h a", a=2),
               bc(C["rowpar"], 1, FH), ALU.mult)
            tt(ES[:, :, :], ES[:, :, :], bc(RR[:, 0:16], 2, KEYS), ALU.mult)
            for j in range(4):
                q.do(V.tensor_copy(PN[32 * j:32 * j + 32, :, 32 * j:32 * j + 32].rearrange("p h (a l) -> p h a l", a=2),
                                   ES[32 * j:32 * j + 32, :, PAST:KEYS].rearrange("p (h a) l -> p h a l", a=2)),
                     S("s_probs") if j == 3 else None)
            q.settle()
            for h in range(FH):
                dve.wait_ge(S("sT_done"), h + 1)
                if h % 2 == 0:
                    dve.wait_ge(S("sT_even"), h // 2 + 1)
                    q.link(V.tensor_copy(stat[:, 15:16], C["eps"]), S("sT_ready"))
                else:
                    if h >= 2:
                        dve.wait_ge(S("so_done"), h - 1)
                    q.link(V.tensor_copy(PT[:, 1, :], PS[:, 1, 0:TOK]), S("sT_ready"))
            dve.wait_ge(S("so_done"), FH)
            q.link(V.tensor_copy(PJ[:, 2, QO:KO], PS[:, 6, :]), S("fox_done"))
            x1 = PJ[:, :, RQO:RVO].rearrange("p t (g h d) -> p t g h d", h=2, d=RK // 2)
            for t in range(NT):
                cos = bc(C["cos"][:, 32 * t:32 * (t + 1)], 1, 2 * RH)
                sin = bc(C["sin"][:, 32 * t:32 * (t + 1)], 1, 2 * RH)
                lo, hi = x1[:, t, :, 0, :], x1[:, t, :, 1, :]
                q.do(V.tensor_tensor(T1[:, t], lo, cos, ALU.mult))
                q.link(V.tensor_tensor(T2[:, t], hi, sin, ALU.mult))
                q.link(V.tensor_tensor(RT[:, t, :, 0:RK // 2], T1[:, t], T2[:, t], ALU.subtract))
                q.do(V.tensor_tensor(T1[:, t], lo, sin, ALU.mult))
                q.link(V.tensor_tensor(T2[:, t], hi, cos, ALU.mult))
                q.link(V.tensor_tensor(RT[:, t, :, RK // 2:RK], T1[:, t], T2[:, t], ALU.add))
            ts(RT[:, :, RH:2 * RH, :], RT[:, :, RH:2 * RH, :], RK ** -0.5, None, ALU.mult, sem=S("rot_ready"))
            dve.wait_ge(S("ret_in"), 32)
            for t in range(2):
                tt(KDP[:, t], RT[:, t, RH:2 * RH, :], bc(RC["kdec_p"], 2, RK), ALU.mult)
            for par in range(2):
                tt(KDS[:, :, par, :], RT[:, 2, RH:2 * RH, :],
                   bc(RC["kdec_s"].rearrange("p (h a) -> p h a", a=2)[:, :, par], 2, RK), ALU.mult)
            for i in range(1, 2 * RH, 2):
                dve.wait_ge(S("ret_tr"), i + 1)
                q.do(V.tensor_copy(QRT[0:RK, i, :], PS[0:RK, i, 0:TOK]), S("qrt_odd"))
            q.settle()
            dve.wait_ge(S("qrt_even"), 4)
            tt(QD1[0:RK], QRT[0:RK, 0:RH, P:2 * P], RC["qdec_p"][0:RK].rearrange("p (h n) -> p h n", h=RH), ALU.mult)
            dve.wait_ge(S("qd2_in"), 1)
            tt(QD2[:, :, :], QD2[:, :, :], RC["qdec_s"].rearrange("p (h n) -> p h n", h=RH), ALU.mult, S("qd_ready"))
            gam = gammas()

            def decay(h):
                dve.wait_ge(S("rs_done"), h + 1)
                if h >= 2:
                    dve.wait_ge(S("y_done"), h - 1)
                q.do(V.tensor_tensor(SD[:, h % 2, 0:SEQ].rearrange("p (t n) -> p t n", t=2),
                                     PS[:, h % 2, 0:SEQ].rearrange("p (t n) -> p t n", t=2),
                                     bc(RC["dec_p"][:, P * h:P * (h + 1)], 1, 2), ALU.mult))
                q.do(V.tensor_tensor(SD[:, h % 2, SEQ:TOK], PS[:, h % 2, SEQ:TOK], RC["dec_s"][:, P * h:P * (h + 1)],
                                     ALU.mult), S("sd_ready"))
                dve.wait_ge(S("sadd_done"), h + 1)
                q.link(V.tensor_copy(S1[0:RK, h, 0, :], PS[0:RK, 4 + h % 2, 0:P]))
                q.link(V.scalar_tensor_tensor(S1[0:RK, h, 1, :], S1[0:RK, h, 0, :], float(gam[h] ** P),
                                              PS[0:RK, 4 + h % 2, P:2 * P], ALU.mult, ALU.add), S("s2_ready"))

            for h in range(RH):
                decay(h)
            for j in range(4):
                dve.wait_ge(S("sstate_done"), j + 1)
                for h in range(RH):
                    q.do(V.scalar_tensor_tensor(STN[:, j, h, :], STt[:, j, h, :], float(gam[h] ** LS),
                                                PS[:, 6 + j % 2, RV * h:RV * (h + 1)], ALU.mult, ALU.add),
                         S("stn_ready") if h == RH - 1 else None)
            q.settle()
            dve.wait_ge(S("yr_ready"), RH)
            yr = YR[:, :, :, :].rearrange("p t h v -> p (t h) v")
            yq = YQ[:, :, :, :].rearrange("p t h v -> p (t h) v")
            red(stat[:, 0:12], yr, ALU.add)
            ts(stat[:, 0:12], stat[:, 0:12], 1.0 / RV, None, ALU.mult)
            tt(yr, yr, bc(stat[:, 0:12], 2, RV), ALU.subtract, S("yr_centred"))
            dve.wait_ge(S("yr_sq"), 1)
            red(stat[:, 0:12], yq, ALU.add, S("yr_sumsq"))
            dve.wait_ge(S("yr_rms"), 1)
            q.link(V.reciprocal(stat[:, 0:12], stat[:, 0:12]))
            tt(yr, yr, bc(stat[:, 0:12], 2, RV), ALU.mult)
            yt = YR[:, :, :, :].rearrange("p t h v -> p t (h v)")
            tt(yt, yt, bc(GN[:, :], 1, NT), ALU.mult)
            dve.wait_ge(S("rg_silu"), 1)
            dve.wait_ge(S("k_stored"), 32)
            tt(PJ[:, :, KO:VO], yt, PJ[:, :, RGO:MIX], ALU.mult, S("mix_ready"))
            stream_odd(1, HT)

            def add_projection(done, base_):
                for u in range(4):
                    dve.wait_ge(S(done), base_ + u + 1)
                    b0 = 2 * (u % 2)
                    xa, xb = X[:, 0:2, UCOL * u:UCOL * (u + 1)], X[:, 2, UCOL * u:UCOL * (u + 1)]
                    q.do(V.tensor_tensor(xa, xa, PS[:, b0, :].rearrange("p (t n) -> p t n", t=2), ALU.add), S("x_mixed"))
                    q.do(V.tensor_tensor(xb, xb, PS[:, b0 + 1, 0:UCOL], ALU.add), S("x_mixed"))
                q.settle()

            add_projection("wout_done", 0)

            def first_max(onehot, vals, best, rank_, tie):
                red(best, vals, ALU.max)
                tt(onehot, vals, bc(best, 2, vals.shape[2]), ALU.is_equal)
                if len(tie.shape) == 2:
                    tie = bc(tie, 1, NT)
                    tt(onehot, onehot, tie, ALU.mult)
                else:
                    for t in range(NT):
                        v = onehot[:, t, :].rearrange("p (g e) -> p g e", g=NG)
                        tt(v, v, tie, ALU.mult)
                red(rank_, onehot, ALU.max)
                tt(onehot, onehot, bc(rank_, 2, vals.shape[2]), ALU.is_equal)

            def moe(lay, stream, base):
                norm_apply(2 * lay + 1, NM)
                q.link(V.tensor_copy(XHI[:, :, :], NM[:, :, :]))
                tt(XLO[:, :, :], NM[:, :, :], XHI[:, :, :].bitcast(F32), ALU.subtract)
                stream_odd(stream - 1, HM)
                dve.wait_ge(S("router_in"), 64 * (lay + 1))
                dve.wait_ge(S("logits_done"), lay + 1)
                tt(LG[:, :, :], PS[:, 0, 0:NT * NR].rearrange("p (t n) -> p t n", t=NT), bc(BR[:, :], 1, NT), ALU.add)
                gl = LG[:, :, 0:NG]
                first_max(OH[:, :, :], gl, R8[:, 0:3], R8[:, 3:6], C["tie"][:, 0:NG])
                tt(E4[:, :, :], gl, bc(R8[:, 0:3], 2, NG), ALU.subtract, S("gl_centred"))
                dve.wait_ge(S("gl_exp"), lay + 1)
                red(R8[:, 6:9], E4[:, :, :], ALU.add)
                q.link(V.reciprocal(R8[:, 9:12], R8[:, 6:9]))
                for t in range(NT):
                    tt(SE[:, t, :].rearrange("p (g e) -> p g e", g=NG), LG[:, t, NG:NR].rearrange("p (g e) -> p g e", g=NG),
                       bc(OH[:, t, :], 2, EPG), ALU.mult)
                ts(E4[:, :, :], OH[:, :, :], -NEG, NEG, ALU.mult, ALU.add)
                for t in range(NT):
                    v = SE[:, t, :].rearrange("p (g e) -> p g e", g=NG)
                    tt(v, v, bc(E4[:, t, :], 2, EPG), ALU.add)
                tie = bc(C["tie"], 1, NG)
                first_max(O1[:, :, :], SE[:, :, :], R8[:, 12:15], R8[:, 3:6], tie)
                q.link(V.scalar_tensor_tensor(SE[:, :, :], O1[:, :, :], 2 * NEG, SE[:, :, :], ALU.mult, ALU.add))
                first_max(O2[:, :, :], SE[:, :, :], R8[:, 15:18], R8[:, 3:6], tie)
                tt(SE[:, :, :], O1[:, :, :], O2[:, :, :], ALU.add, S("chosen"))
                tt(R8[:, 18:21], R8[:, 15:18], R8[:, 12:15], ALU.subtract, S("d_ready"))
                dve.wait_ge(S("d_exp"), lay + 1)
                ts(R8[:, 24:27], R8[:, 21:24], 1.0, None, ALU.add)
                q.link(V.reciprocal(R8[:, 24:27], R8[:, 24:27]))
                tt(R8[:, 27:30], R8[:, 24:27], R8[:, 9:12], ALU.mult)
                tt(R8[:, 30:33], R8[:, 27:30], R8[:, 21:24], ALU.mult)
                tt(O1[:, :, :], O1[:, :, :], bc(R8[:, 27:30], 2, NE), ALU.mult)
                tt(O2[:, :, :], O2[:, :, :], bc(R8[:, 30:33], 2, NE), ALU.mult)
                tt(WG[:, :, :], O1[:, :, :], O2[:, :, :], ALU.add)
                dve.wait_ge(S("ranks_done"), lay + 1)
                ts(SL[:, :, :], PS[:, 1, 0:NT * NE].rearrange("p (t n) -> p t n", t=NT), 1.0, None, ALU.add)
                q.link(V.tensor_reduce(out=R8[:, 33:34], in_=PS[:, 1, NT * NE:(NT + 1) * NE], axis=AXX, op=ALU.max))
                tt(SL[:, :, :], SL[:, :, :], SE[:, :, :], ALU.mult)
                for w in range(MAXWIN):
                    for t in range(NT):
                        dst = SV[:, NQ * w:NQ * (w + 1), QUAD * t:QUAD * (t + 1)]
                        q.do(V.tensor_scalar(dst, SL[:, t, :].rearrange("p (q e) -> p q e", e=QUAD), -1.0 - CAP * w, None,
                                             ALU.add))
                        dst = WV[:, NQ * w:NQ * (w + 1), QUAD * t:QUAD * (t + 1)]
                        q.do(V.tensor_copy(dst, WG[:, t, :].rearrange("p (q e) -> p q e", e=QUAD)))
                q.settle()
                ts(R8[:, 34:39], C["iota"][:, 1:MAXWIN], float(CAP), None, ALU.mult)
                ts(R8[:, 34:39], R8[:, 34:39], R8[:, 33:34], None, ALU.is_lt)
                red(R8[:, 39:40], R8[:, 34:39], ALU.add)
                ts(NW[:, lay:lay + 1], R8[:, 39:40], float(NQ), None, ALU.mult, sem=S("steps_known"))
                n = dve.value_load(NW[0:1, lay:lay + 1], min_val=0, max_val=(MAXWIN - 1) * NQ) + NQ
                if lay == 0:
                    dve.sem_inc(S("hid_ready"), 2)
                    dve.sem_inc(S("yl_ready"), 2)
                    dve.sem_inc(S("x_added"), 6)

                def onehot(s):
                    V.tensor_tensor(G[:, :, :], bc(C["iota"], 1, NT * QUAD),
                                    bc(SV[:, bass.ds(s, 1), :].rearrange("p o n -> p (o n)"), 2, CAP),
                                    ALU.is_equal).then_inc(S("g_ready"), 1)

                def weighted(s):
                    dve.wait_ge(S("g_ready"), base + s + 1)
                    V.tensor_tensor(GW[:, :, :], G[:, :, :].bitcast(F32),
                                    bc(WV[:, bass.ds(s, 1), :].rearrange("p o n -> p (o n)"), 2, CAP),
                                    ALU.mult).then_inc(S("gw_ready"), 1)

                def step(s, more):
                    g = base + s

                    def hidden(pair):
                        dve.wait_ge(S("silu_ready"), g * 2 + (pair + 1))
                        V.tensor_tensor(HID[:, pair, :, :, :].rearrange("p e j n -> p (e j n)"),
                                        PS[:, 2 + pair, 4 * CAP:8 * CAP],
                                        SG[:, pair, :, :].rearrange("p e n -> p (e n)"),
                                        ALU.mult).then_inc(S("hid_ready"), 1)

                    hidden(0)
                    if more:
                        dve.wait_ge(S("gathered"), g * 2 + 2)
                        dve.wait_ge(S("gw_ready"), g + 1)
                        onehot(s + 1)
                    for pair in range(2):
                        dve.wait_ge(S("gw_tr"), g * 2 + (pair + 1))
                        V.tensor_scalar(GT[:, pair, :], PS[:, 6 + pair, 0:TOK], 0.0, None,
                                        ALU.is_gt).then_inc(S("gt_ready"), 1)
                        V.tensor_reduce(out=GATE[:, pair:pair + 1], in_=PS[:, 6 + pair, 0:TOK], axis=AXX,
                                        op=ALU.add).then_inc(S("gt_ready"), 1)
                    hidden(1)
                    if more:
                        weighted(s + 1)
                    for pair in range(2):
                        dve.wait_ge(S("yh_ready"), g * 2 + (pair + 1))
                        dve.wait_ge(S("gt_ready"), g * 4 + (2 * pair + 2))
                        V.scalar_tensor_tensor(YL[:, pair, :], PS[:, 4:6, :].rearrange("p a n -> p (a n)"),
                                               GATE[:, pair:pair + 1], YH[:, pair, :].bitcast(F32), ALU.mult,
                                               ALU.subtract).then_inc(S("yl_ready"), 1)
                    for i in range(2 * NT):
                        t, h = divmod(i, 2)
                        dve.wait_ge(S("sum_done"), g * 6 + (i + 1))
                        v = X[:, t, 512 * h:512 * (h + 1)]
                        V.tensor_tensor(v, v, PS[:, 6 + i % 2, :], ALU.add).then_inc(S("x_added"), 1)

                dve.wait_ge(S("steps_known"), lay + 1)
                onehot(0)
                weighted(0)
                with dve.Fori(0, n - 1) as s:
                    step(s, True)
                step(n - 1, False)
                dve.wait_ge(S("x_added"), (base + n) * 6 + 6)
                q.link(V.tensor_copy(stat[:, 14:15], C["eps"]), S("moe_done"))
                return n

            steps0 = moe(0, 3, 0)
            norm_apply(2, NC)
            q.link(V.memset(U[:, :, 0:HIST], 0.0))
            stream_odd(3, HC)
            dve.wait_ge(S("hist_ready"), KD)
            dve.wait_ge(S("taps_ready"), 2)
            for c in range(KD):
                dve.wait_ge(S("sig_ready"), c + 1)
                u_p = U[:, c, 0:HIST + SEQ]
                u_s = U[:, c, HIST + SEQ:WID].rearrange("p (b w) -> p b w", b=NS)
                pa = PS[:, 2 * (c % 2), 0:TOK]
                q.do(V.scalar_tensor_tensor(u_p[:, HIST:], pa[:, 0:SEQ], SMT[:, c:c + 1], SGC[:, c % 2, 0:SEQ],
                                            ALU.add, ALU.mult))
                q.do(V.scalar_tensor_tensor(u_s[:, :, HIST:], pa[:, SEQ:TOK].rearrange("p (b l) -> p b l", b=NS),
                                            SMT[:, c:c + 1], SGC[:, c % 2, SEQ:TOK].rearrange("p (b l) -> p b l", b=NS),
                                            ALU.add, ALU.mult), S("u_ready"))
                q.settle()
                bank = 4 + c % 2
                accp = PS[:, bank, 0:SEQ]
                accs = PS[:, bank, SEQ:TOK].rearrange("p (b l) -> p b l", b=NS)
                yp = YC[:, c, 0:SEQ]
                ys = YC[:, c, SEQ:TOK].rearrange("p (b l) -> p b l", b=NS)
                for w in range(CONV_W):
                    last = w == CONV_W - 1
                    tap = WDT[:, c, w:w + 1]
                    for part, (src, acc, y) in enumerate(((u_p[:, w:w + SEQ], accp, yp), (u_s[:, :, w:w + LS], accs, ys))):
                        sem = S("y_conv") if last and part else S("conv_p" if part == 0 else "conv_s")
                        if w:
                            prev = S("conv_p" if part == 0 else "conv_s")
                            dve.wait_ge(prev, q.count[id(prev)])
                        if w == 0:
                            ins = V.tensor_scalar(acc, src, tap, SMT[:, 16 + c:17 + c], ALU.mult, ALU.add)
                        else:
                            ins = V.scalar_tensor_tensor(y if last else acc, src, tap, acc, ALU.mult, ALU.add)
                        q.do(ins, sem)
            q.settle()
            dve.wait_ge(S("mean_done"), 1)
            tt(YC[:, :, :], YC[:, :, :], bc(PS[:, 6, 0:TOK], 1, KD), ALU.subtract, S("yc_centred"))
            dve.wait_ge(S("cstd_ready"), 1)
            q.link(V.reciprocal(VR[:, :], VR[:, :]))
            dve.wait_ge(S("ysq_ready"), 1)
            tt(YC[:, :, :], YC[:, :, :], bc(VR[:, :], 1, KD), ALU.mult, S("yc_normed"))
            add_projection("pw_done", 8)
            moe(1, 5, steps0)


INPUTS = ["x_prompt", "x_sample", "cache_fox_k", "cache_fox_v", "cache_fox_logf", "state_ret", "cache_conv",
          "norm_mix", "norm_ffn", "w_in_mix", "b_forget", "fox_q_gain", "fox_k_gain", "ret_gn_gain", "w_out_mix",
          "w_pw1", "b_pw1", "w_dw", "b_dw", "conv_ln_g", "conv_ln_b", "w_pw2", "w_router_group", "b_router_group",
          "w_router_expert", "b_router_expert", "w_exp_gate", "w_exp_up", "w_exp_down"]
OUTPUTS = [("y_prompt", (1, SEQ, D)), ("y_sample", (NS, LS, D)), ("fox_k_prompt", (1, 1, SEQ, FH, FD)),
           ("fox_v_prompt", (1, 1, SEQ, FH, FD)), ("fox_logf_prompt", (1, 1, SEQ, FH)),
           ("ret_state_prompt", (1, 1, RH, RK, RV)), ("conv_prompt", (1, 1, HIST, D)),
           ("fox_k_sample", (1, NS, LS, FH, FD)), ("fox_v_sample", (1, NS, LS, FH, FD)),
           ("fox_logf_sample", (1, NS, LS, FH)), ("ret_state_sample", (1, NS, RH, RK, RV)),
           ("conv_sample", (1, NS, HIST, D))]


def kernel(**inputs):
    import concourse.bacc as bacc
    from concourse.bass_utils import run_bass_kernel_spmd

    nc = bacc.Bacc("TRN2", target_bir_lowering=False, num_devices=1)
    cst, rcst, head = constants()
    arrays = {name: np.ascontiguousarray(inputs[name]) for name in INPUTS}
    arrays.update(cst=cst, rcst=rcst, head=head)
    a = {name: nc.dram_tensor(f"in_{name}", x.shape, F32, kind="ExternalInput").ap() for name, x in arrays.items()}
    o = {name: nc.dram_tensor(f"out_{name}", shape, F32, kind="ExternalOutput").ap() for name, shape in OUTPUTS}
    build(nc, a, o)
    r = run_bass_kernel_spmd(nc, [{f"in_{name}": x for name, x in arrays.items()}], core_ids=[0])
    return tuple(r.results[0][f"out_{name}"] for name, _ in OUTPUTS)
```

```python
from contextlib import ExitStack

import numpy as np

import concourse.bass as bass
from concourse import mybir

F32 = mybir.dt.float32
F32R = mybir.dt.float32r
I32 = mybir.dt.int32
ALU = mybir.AluOpType
ACT = mybir.ActivationFunctionType
AXX = mybir.AxisListType.X

P = 128
D = 1024
KD = D // P
NT = 3
TOK = NT * P
SEQ, NS, LS, PAST = 256, 8, 16, 128
FH, FD = 8, 64
RH, RK, RV = 4, 64, 128
MIX = 3 * FH * FD + 2 * RH * RK + 2 * RH * RV
QO, KO, VO = 0, FH * FD, 2 * FH * FD
FF_COL = 3 * FH * FD
RQO = 3 * FH * FD
RVO = RQO + 2 * RH * RK
RGO = RVO + RH * RV
KEYS = PAST + LS
CONV_W, HIST = 31, 30
NG, EPG, NE, FE = 4, 8, 32, 256
NR = NG + NE
CAP = 64
QUAD = 4
NQ = NE // QUAD
MAXWIN = TOK // CAP
EPS = 1e-6
MIX_LOADS = 6 + NS
STATE_STORES = 1 + NS
CONV_STORES = 1 + NS
NEG = -1e30
NBLK = TOK // LS
PBLK = SEQ // LS
POOL_TAPS = 11
UNIT = 2048
LO, HI = 6, 12
NEAR = 6
UCOL = 256


def gammas():
    return 1.0 - 2.0 ** (-5.0 - np.arange(RH, dtype=np.float64))


def layout(parts):
    at, n = {}, 0
    for name, width in parts:
        at[name] = (n, n + width)
        n += width
    return at, n


CONSTS, CONST_W = layout([
    ("ident", P), ("tri", P), ("strict", P), ("ones", P), ("blk", P), ("mask", 2 * P), ("smask", KEYS),
    ("rowpar", 2), ("sel", P + P - LS), ("cos", NT * 32), ("sin", NT * 32), ("iota", CAP), ("tie", EPG),
    ("onesd", P), ("eps", 1)])
RCONSTS, RCONST_W = layout([
    ("dec_p", RH * P), ("dec_s", RH * P), ("kdec_p", RH), ("kdec_s", 2 * RH), ("qdec_p", RH * P),
    ("qdec_s", RH * P)])


def constants():
    p = np.arange(P)
    c = np.zeros((P, CONST_W), np.float64)

    def put(name, a):
        a0, a1 = CONSTS[name]
        c[:, a0:a1] = np.asarray(a, np.float64).reshape(P, a1 - a0)

    k, m = p[:, None], p[None, :]
    put("ident", k == m)
    put("tri", k <= m)
    put("strict", k < m)
    put("ones", np.ones((P, P)))
    put("blk", (k <= m) & (k // LS == m // LS))
    put("mask", np.concatenate([np.zeros((P, P)), np.where(m <= k, 0.0, NEG)], 1))
    j = np.arange(KEYS)[None, :]
    put("smask", np.where((j < PAST) | (j - PAST <= k % LS), 0.0, NEG))
    par = (p // LS) % 2
    put("rowpar", np.stack([par == 0, par == 1], 1))
    sel = np.zeros((P, P + P - LS))
    sel[:, P - LS:P] = 1.0
    put("sel", sel)
    pos = np.stack([p, P + p, PAST + p % LS], 1).astype(np.float32)
    freq = (np.float32(10000.0) ** (-np.arange(32, dtype=np.float32) / np.float32(32))).astype(np.float32)
    ang = (pos[:, :, None] * freq[None, None, :]).astype(np.float32).astype(np.float64)
    put("cos", np.cos(ang))
    put("sin", np.sin(ang))
    put("iota", np.broadcast_to(np.arange(CAP), (P, CAP)))
    put("tie", np.broadcast_to(EPG - np.arange(EPG), (P, EPG)))
    put("onesd", np.full((P, P), 1.0 / D))
    put("eps", np.full((P, 1), EPS))
    g = gammas()
    r = np.zeros((P, RCONST_W), np.float64)

    def putr(name, a):
        a0, a1 = RCONSTS[name]
        r[:, a0:a1] = np.asarray(a, np.float64).reshape(P, a1 - a0)

    diff = np.maximum(m - k, 0)
    idx = p % LS
    putr("dec_p", np.stack([np.where(k <= m, gg ** diff, 0.0) for gg in g], 1))
    putr("dec_s", np.stack([np.where((k <= m) & (k // LS == m // LS), gg ** diff, 0.0) for gg in g], 1))
    putr("kdec_p", np.stack([gg ** (P - 1.0 - p) for gg in g], 1))
    putr("kdec_s", np.stack([np.where(par == q, gg ** (LS - 1.0 - idx), 0.0) for gg in g for q in (0, 1)], 1))
    putr("qdec_p", np.broadcast_to(np.stack([gg ** (p + 1.0) for gg in g], 0)[None], (P, RH, P)))
    half = (p // RK)[:, None, None]
    putr("qdec_s", np.where(par[None, None, :] == half, np.stack([gg ** (idx + 1.0) for gg in g], 0)[None], 0.0))
    head = np.zeros((FH, FH, TOK))
    for h in range(FH):
        head[h, h] = 1.0
    return c.astype(np.float32), r.astype(np.float32), head.reshape(FH, FH * TOK).astype(np.float32)


class InOrder:

    def __init__(self, eng, own):
        self.eng, self.own, self.count, self.open = eng, own, {}, {}

    def do(self, ins, sem=None):
        sem = self.own if sem is None else sem
        n = self.count.get(id(sem), 0) + 1
        self.count[id(sem)] = n
        self.open[id(sem)] = (sem, n)
        ins.then_inc(sem, 1)

    def settle(self):
        for sem, n in self.open.values():
            self.eng.wait_ge(sem, n)
        self.open = {}

    def link(self, ins, sem=None):
        self.do(ins, sem)
        self.settle()


def bc(ap, dim, n):
    shape = list(ap.shape)
    return ap.unsqueeze(dim).to_broadcast(shape[:dim] + [n] + shape[dim:])


def build(nc, a, o):
    with ExitStack() as ctx:
        sems = {}

        def S(name):
            if name not in sems:
                sems[name] = ctx.enter_context(nc.semaphore(name))
            return sems[name]

        class Region:
            def __init__(self, start, end):
                self.n, self.end = start, end

            def __call__(self, name, shape, dt=F32):
                off = self.n
                self.n += (int(np.prod(shape[1:])) * 4 + 31) // 32 * 32
                assert self.n <= self.end, (name, self.n, self.end)
                return nc.alloc_sbuf_tensor_at(name, shape, dt, offset=off)

        limit = nc.sbuf_usable_end // 32 * 32
        keep = Region((nc.sbuf_base + 31) // 32 * 32, limit)
        X = keep("X", [P, NT, D])
        cst = keep("cst", [P, CONST_W])
        gb = keep("gain_rows", [P, D])
        stat = keep("stat", [P, 16])
        NW = keep("steps", [P, 8], I32)
        slot = [keep(f"slot{i}", [P, UNIT]) for i in range(LO)]
        hi_at = keep.n
        slot += [keep(f"slot{i}", [P, UNIT]) for i in range(LO, HI)]
        arena = keep.n
        C = {n: cst[:, x0:x1] for n, (x0, x1) in CONSTS.items()}
        ident = C["ident"]

        rh = Region(hi_at, arena)
        PJ = rh("PJ", [P, NT, MIX])
        STt = rh("STt", [P, 4, RH, RV])
        FF = rh("FF", [P, NT, FH])
        LF = rh("LF", [P, NT, FH])
        LT = rh("LT", [P, NT, FH])
        CQ = rh("CQ", [P, NT, FH])
        CLF = rh("CLF", [P, NS, FH])
        WF = rh("WF", [P, KD, FH])
        GQ = rh("GQ", [P, FD])
        GK = rh("GK", [P, FD])
        BF = rh("BF", [P, FH])
        MS = rh("MS", [P, NT * FH])
        MX = rh("MX", [P, 16])
        SM = rh("SM", [P, 16])
        RR = rh("RR", [P, 16])
        ra = Region(arena, limit)
        HT = ra("HT", [P, KD, TOK])
        QT = ra("QT", [P, FH, TOK])
        KT = ra("KT", [P, FH, TOK])
        over = Region(ra.n, limit)
        HN = over("HN", [P, NT, D])
        SQ = over("SQ", [P, NT, FH * FD])
        over = Region(ra.n, limit)
        PN = over("PN", [P, FH, P])
        KTC = ra("KTC", [P, NS, FH, KEYS])
        over = Region(ra.n, limit)
        SS = over("SS", [P, 2, TOK])
        ES = ra("ES", [P, FH * 2, KEYS])
        PT = ra("PT", [P, 2, TOK])
        over = Region(arena, limit)
        YQ = over("YQ", [P, NT, RH, RV])
        rr = Region(arena + TOK * KD * 4, limit)
        rcst = rr("rcst", [P, RCONST_W])
        RT = rr("RT", [P, NT, 2 * RH, RK])
        T1 = rr("T1", [P, NT, 2 * RH, RK // 2])
        T2 = rr("T2", [P, NT, 2 * RH, RK // 2])
        QRT = rr("QRT", [P, 2 * RH, TOK])
        SD = rr("SD", [P, 2, TOK])
        QD1 = rr("QD1", [P, RH, P])
        QD2 = rr("QD2", [P, RH, P])
        KDP = rr("KDP", [P, 2, RH, RK])
        KDS = rr("KDS", [P, RH, 2, RK])
        S1 = rr("S1", [P, RH, 2, RV])
        STN = rr("STN", [P, 4, RH, RV])
        VM = rr("VM", [P, 4, RH * RV])
        YR = rr("YR", [P, NT, RH, RV])
        GN = rr("GN", [P, RH * RV])
        RC = {n: rcst[:, x0:x1] for n, (x0, x1) in RCONSTS.items()}

        rm = Region(arena, limit)
        XHI = rm("XHI", [P, NT, D], F32R)
        XLO = rm("XLO", [P, NT, D], F32R)
        XG = rm("XG", [P, KD, QUAD * CAP])
        G = rm("G", [P, NT * QUAD, CAP], F32R)
        GW = rm("GW", [P, NT * QUAD, CAP])
        GT = rm("GT", [P, 2, TOK], F32R)
        over = Region(rm.n, limit)
        NM = over("NM", [P, NT, D])
        YH = rm("YH", [P, 2, D], F32R)
        YL = rm("YL", [P, 2, D], F32R)
        SG = rm("SG", [P, 2, FE])
        HT2 = rm("hid_by_token", [P, 2, FE])
        HID = rm("HID", [P, 2, 2, 2, CAP])
        SV = rm("SV", [P, MAXWIN * NQ, NT * QUAD])
        WV = rm("WV", [P, MAXWIN * NQ, NT * QUAD])
        GATE = rm("GATE", [P, 2])
        HM = rm("HM", [P, KD, TOK])
        WR = rm("WR", [P, KD, NR])
        BR = rm("BR", [P, NR])
        LG = rm("LG", [P, NT, NR])
        OH = rm("OH", [P, NT, NG])
        E4 = rm("E4", [P, NT, NG])
        FAR = rm("FAR", [P, NT, NG])
        EQ = rm("EQ", [P, NT, NE])
        SE = rm("SE", [P, NT, NE])
        O1 = rm("O1", [P, NT, NE])
        O2 = rm("O2", [P, NT, NE])
        WG = rm("WG", [P, NT, NE])
        SL = rm("SL", [P, NT, NE])
        R8 = rm("R8", [P, 48])

        rc = Region(arena, limit)
        over = Region(rc.n, limit)
        YS = over("YS", [P, KD, TOK])
        HC = rc("HC", [P, KD, TOK])
        U = rc("U", [P, KD, NBLK, HIST + LS])
        over = Region(rc.n, limit)
        NC = over("NC", [P, NT, D])
        YC = rc("YC", [P, KD, TOK])
        YD = rc("YD", [P, TOK])
        YP = rc("YP", [P, 2, TOK])
        VR = rc("VR", [P, TOK])
        SGC = rc("SGC", [P, 2, TOK])
        over = Region(rc.n, limit)
        UN = over("UN", [P, KD, P])
        PR = over("PR", [P, 2, TOK])
        CC = rc("CC", [P, 2, D])
        WDR = rc("WDR", [P, D])
        WDT = rc("WDT", [P, KD, CONV_W])
        SMR = rc("SMR", [P, P])
        SMT = rc("SMT", [P, 40])
        CS = rc("CS", [P, D])
        CP = rc("CP", [P, D])

        PS = nc.alloc_psum_tensor("PS", [P, 8, 512], F32)

        xp = a["x_prompt"].rearrange("b (t p) d -> p (b t) d", p=P)
        xs = a["x_sample"].rearrange("b l d -> (b l) d")
        w_in = a["w_in_mix"].rearrange("l (p k) n -> p (l k) n", k=KD)
        w_out = a["w_out_mix"].rearrange("l (p k) n -> p (l k) n", k=KD)
        w_pw1 = a["w_pw1"].rearrange("l (p k) n -> p (l k) n", k=KD)
        w_pw2 = a["w_pw2"].rearrange("l (k p) n -> p (l k) n", k=KD)
        w_gate = a["w_exp_gate"].rearrange("l g e (p k) f -> (l g e) p (k f)", k=KD)
        w_up = a["w_exp_up"].rearrange("l g e (p k) f -> (l g e) p (k f)", k=KD)
        w_down = a["w_exp_down"].rearrange("l g e (j p) n -> (l g e) p j n", p=P)

        def row(ap, n):
            return ap.rearrange("(o n) -> o n", o=1).to_broadcast([P, n])

        def cols(u):
            return UCOL * u + (FH if u >= FF_COL // UCOL else 0)

        def dense(i):
            return slot[i % LO][:, :].rearrange("p (k n) -> p k n", k=KD)

        N_IN = MIX // UCOL
        block = ctx.enter_context(nc.Block())

        @block.sync
        def _(sp):
            for t in range(2):
                sp.dma_start(X[:, t, :], xp[:, t, :]).then_inc(S(f"x_in{t}"), 16)
            sp.dma_start(X[:, 2, :], xs).then_inc(S("x_in2"), 16)
            sp.dma_start(cst[:, :], a["cst"]).then_inc(S("cst_in"), 16)
            sp.dma_start(gb[:, :], row(a["norm_mix"][0], D)).then_inc(S("gain0_in"), 16)

            def unit(seg, i):
                return dense(i), S(f"{seg}_full{i % LO}")

            for i in range(N_IN):
                if i >= LO:
                    sp.wait_ge(S("proj_done"), i - LO + 1)
                dst, full = unit("a", i)
                sp.dma_start(dst, w_in[:, :, cols(i):cols(i) + UCOL]).then_inc(full, 16)
            for i in range(4):
                sp.wait_ge(S("proj_done"), LO + i + 1)
                src = a["cache_fox_k" if i < 2 else "cache_fox_v"]
                src = src[0, 4 * (i % 2):4 * (i % 2) + 4].rearrange("b p h d -> p b (h d)")
                n = N_IN + i
                sp.dma_start(slot[n % LO][:, :].rearrange("p (b c) -> p b c", b=4), src).then_inc(
                    S(f"a_full{n % LO}"), 16)
            for i in range(4):
                if i < 2:
                    sp.wait_ge(S("proj_done"), N_IN - 1 + i)
                else:
                    sp.wait_ge(S("cachek_tr"), 4 * (i - 1))
                dst, full = unit("a", N_IN + 4 + i)
                sp.dma_start(dst, w_out[:, :, UCOL * i:UCOL * i + UCOL]).then_inc(full, 16)

            def expert_loads(lay, q, before, order=range(HI)):
                for n in order:
                    before(n)
                    if n < 8:
                        e = n // 2
                        src = (w_gate, w_up)[n % 2][bass.ds(q * QUAD + (lay * NE + e), 1)]
                        sp.dma_start(slot[n][:, :], src.rearrange("o p n -> p (o n)")).then_inc(
                            S(f"gu_full{e}"), 16)
                    else:
                        e = n - 8
                        src = w_down[bass.ds(q * QUAD + (lay * NE + e), 1)]
                        sp.dma_start(slot[n][:, :].rearrange("p (j n) -> p j n", j=2),
                                     src.rearrange("o p j n -> p (o j) n")).then_inc(S(f"d_full{e}"), 16)

            def used(n, s):
                if n < 8:
                    sp.wait_ge(S("gu_done"), s * 2 + (n // 4 - 1))
                else:
                    sp.wait_ge(S("d_done"), s * 2 + (n // 10 - 1))

            def expert_loop(lay, base, n):
                with sp.Fori(base + 1, base + n) as s:
                    expert_loads(lay, s % NQ, lambda j: used(j, s))

            def first_a(n):
                if n < 2:
                    sp.wait_ge(S("wout_done"), 3 + n)
                elif n < 4:
                    sp.wait_ge(S("so_done"), FH)
                elif n < LO:
                    sp.wait_ge(S("wout_done"), n - 3)
                else:
                    sp.wait_ge(S("tr_done"), 2 * KD)
                    sp.wait_ge(S("mix_stored"), 16 * 5)
            expert_loads(0, 0, first_a, (2, 3, 6, 7, 8, 9, 10, 11, 4, 5, 0, 1))
            sp.wait_ge(S("steps_known"), 1)
            n0 = sp.value_load(NW[0:1, 0:1], min_val=0, max_val=(MAXWIN - 1) * NQ) + NQ
            expert_loop(0, 0, n0)

            for i in range(12):
                if i < LO:
                    used(i, n0)
                else:
                    sp.wait_ge(S("glu_done"), 2 * ((i - LO) // 2) + 2)
                dst, full = unit("c", i)
                if i < 8:
                    c0 = D * (i % 2) + UCOL * (i // 2)
                    sp.dma_start(dst, w_pw1[:, :, c0:c0 + UCOL]).then_inc(full, 16)
                else:
                    sp.dma_start(dst, w_pw2[:, :, UCOL * (i - 8):UCOL * (i - 7)]).then_inc(full, 16)

            def first_c(n):
                if n < 2:
                    sp.wait_ge(S("glu_done"), KD)
                elif n < LO:
                    sp.wait_ge(S("pw_done"), n - 1)
                else:
                    used(n, n0)
            expert_loads(1, 0, first_c, (6, 7, 8, 9, 10, 11, 0, 1, 2, 3, 4, 5))
            sp.wait_ge(S("steps_known"), 2)
            n1 = sp.value_load(NW[0:1, 1:2], min_val=0, max_val=(MAXWIN - 1) * NQ) + NQ
            expert_loop(1, n0, n1)
            yp = o["y_prompt"].rearrange("b (t p) d -> p (b t) d", p=P)
            for t in range(NT):
                sp.wait_ge(S("x_added"), (n0 + n1) * 6 + (2 * t + 2))
                dst = yp[:, t, :] if t < 2 else o["y_sample"].rearrange("b l d -> (b l) d")
                sp.dma_start(dst, X[:, t, :]).then_inc(S("y_stored"), 16)
            sp.wait_ge(S("y_stored"), 16 * NT)

        @block.gpsimd
        def _(pool):
            for dst, src in ((CLF[:, :, :], a["cache_fox_logf"][0].rearrange("b p h -> p b h")),
                             (WF[:, :, :], w_in[:, :, FF_COL:FF_COL + FH]),
                             (GQ[:, :], row(a["fox_q_gain"][0], FD)), (GK[:, :], row(a["fox_k_gain"][0], FD)),
                             (BF[:, :], row(a["b_forget"][0], FH)),
                             (QT[FD:FD + FH, :, :], a["head"].rearrange("c (h t) -> c h t", h=FH))):
                pool.dma_start(dst, src).then_inc(S("mix_in"), 16)
            for b in range(NS):
                pool.dma_start(STt[RK * (b % 2):RK * (b % 2 + 1), b // 2, :, :],
                               a["state_ret"][0, b].rearrange("h d v -> d h v")).then_inc(S("mix_in"), 16)

            def store(dst, src, sem="stored"):
                pool.dma_start(dst, src).then_inc(S(sem), 16)

            tiles = "b (t p) h d -> p (b t) (h d)"
            flat = "b l h d -> (b l) (h d)"
            pool.wait_ge(S("k_ready"), 1)
            store(o["fox_k_prompt"][0].rearrange(tiles, p=P), PJ[:, 0:2, KO:VO], "k_stored")
            store(o["fox_k_sample"][0].rearrange(flat), PJ[:, 2, KO:VO], "k_stored")
            pool.wait_ge(S("lf_ready"), 1)
            store(o["fox_logf_prompt"][0].rearrange("b (t p) h -> p (b t) h", p=P), LF[:, 0:2, :], "mix_stored")
            store(o["fox_logf_sample"][0].rearrange("b l h -> (b l) h"), LF[:, 2, :], "mix_stored")
            pool.wait_ge(S("pj_ready"), N_IN)
            store(o["fox_v_prompt"][0].rearrange(tiles, p=P), PJ[:, 0:2, VO:RQO], "mix_stored")
            store(o["fox_v_sample"][0].rearrange(flat), PJ[:, 2, VO:RQO], "mix_stored")
            pool.wait_ge(S("hn_ready"), NT)
            pool.dma_start(gb[:, :], row(a["norm_ffn"][0], D)).then_inc(S("gain_in"), 16)
            pool.wait_ge(S("s_done"), FH)
            pool.dma_start(rcst[:, :], a["rcst"]).then_inc(S("ret_in"), 16)
            pool.wait_ge(S("fox_done"), 1)
            pool.dma_start(GN[:, :], row(a["ret_gn_gain"][0], RH * RV)).then_inc(S("ret_in"), 16)
            nc.gpsimd.memset(VM[:, :, :], 0.0).then_inc(S("vm_zero"), 1)
            pool.wait_ge(S("s2_ready"), RH)
            store(o["ret_state_prompt"][0, 0].rearrange("h d v -> d h v"), S1[0:RK, :, 1, :])
            pool.wait_ge(S("stn_ready"), 4)
            for b in range(NS):
                store(o["ret_state_sample"][0, b].rearrange("h d v -> d h v"),
                      STN[RK * (b % 2):RK * (b % 2 + 1), b // 2, :, :])
            store(o["conv_sample"][0, :, 0:HIST - LS, :], a["cache_conv"][0, :, LS:HIST, :], "mix_stored")
            pool.wait_ge(S("stored"), 16 * STATE_STORES)
            for lay in range(2):
                pool.wait_ge(S("x_mixed"), 8 * (lay + 1))
                pool.dma_start(WR[:, :, 0:NG], a["w_router_group"][lay].rearrange("(p k) n -> p k n", k=KD)
                               ).then_inc(S("router_in"), 16)
                pool.dma_start(WR[:, :, NG:NR], a["w_router_expert"][lay].rearrange("(p k) n -> p k n", k=KD)
                               ).then_inc(S("router_in"), 16)
                pool.dma_start(BR[:, 0:NG], row(a["b_router_group"][lay], NG)).then_inc(S("router_in"), 16)
                pool.dma_start(BR[:, NG:NR], row(a["b_router_expert"][lay], NE)).then_inc(S("router_in"), 16)
                if lay == 0:
                    pool.wait_ge(S("hn_ready"), 2 * NT)
                    pool.dma_start(gb[:, :], row(a["norm_mix"][1], D)).then_inc(S("gain_in"), 16)
                    pool.wait_ge(S("moe_done"), 1)
                    pool.dma_start(CC[0:120, 0, :], a["cache_conv"][0, 0:4].rearrange("b t c -> (b t) c")
                                   ).then_inc(S("conv_in"), 16)
                    pool.dma_start(CC[0:120, 1, :], a["cache_conv"][0, 4:8].rearrange("b t c -> (b t) c")
                                   ).then_inc(S("conv_in"), 16)
                    pool.dma_start(WDR[0:CONV_W, :], a["w_dw"][0]).then_inc(S("conv_in"), 16)
                    pool.dma_start(SMR[0:16, :], a["b_pw1"][0].rearrange("(c p) -> c p", p=P)
                                   ).then_inc(S("conv_in"), 16)
                    for i, name in enumerate(("b_dw", "conv_ln_g", "conv_ln_b")):
                        pool.dma_start(SMR[16 + 8 * i:24 + 8 * i, :], a[name][0].rearrange("(c p) -> c p", p=P)
                                       ).then_inc(S("conv_in"), 16)
                    pool.wait_ge(S("hn_ready"), 3 * NT)
                    pool.dma_start(gb[:, :], row(a["norm_ffn"][1], D)).then_inc(S("gain_in"), 16)
                    for c in range(KD):
                        acc = YP[:, c % 2, :]
                        pool.wait_ge(S("first_product"), c + 1)
                        for w in range(1, POOL_TAPS):
                            n = c * (POOL_TAPS - 1) + w
                            pool.wait_ge(S("product_ready"), n)
                            if n > 1:
                                pool.wait_ge(S("pool_tap"), n - 1)
                            nc.gpsimd.tensor_tensor(acc, acc, PR[:, (n - 1) % 2, :], ALU.add).then_inc(S("pool_tap"), 1)
                    pool.wait_ge(S("ctok_ready"), 2)
                    store(o["conv_prompt"][0, 0], CP[0:HIST, :])
                    for b in range(NS):
                        store(o["conv_sample"][0, b, HIST - LS:HIST, :], CS[LS * b:LS * (b + 1), :])
                    pool.wait_ge(S("stored"), 16 * (STATE_STORES + CONV_STORES))
            pool.wait_ge(S("k_stored"), 32)
            pool.wait_ge(S("mix_stored"), 16 * 5)

        @block.tensor
        def _(pe):
            mm = nc.tensor.matmul

            def full(seg, i):
                pe.wait_ge(S(f"{seg}_full{i % LO}"), 16 * (i // LO + 1))

            def transpose_stream(src):
                for k in range(KD):
                    for t in range(NT):
                        v = src[:, t, 0:D].rearrange("p (q k) -> p k q", k=KD)[:, k, :]
                        last = nc.tensor.transpose(PS[:, k, P * t:P * (t + 1)], v, ident)
                    last.then_inc(S("tr_done"), 1)

            def wait_stream(n):
                pe.wait_ge(S("tr_even"), 4 * n)
                pe.wait_ge(S("tr_odd"), 4 * n)

            pe.wait_ge(S("cst_in"), 16)
            pe.wait_ge(S("hn_ready"), NT)
            transpose_stream(HN)
            wait_stream(1)
            def project_in(u, t):
                w = dense(u)
                b0 = 2 * (u % 4) if u < NEAR else 6
                if t == 0:
                    full("a", u)
                    if u >= NEAR:
                        pe.wait_ge(S("pj_ready"), u)
                    elif u >= 4:
                        pe.wait_ge(S("pj_ready"), u - 3)
                    if u == FF_COL // UCOL - 1:
                        pe.wait_ge(S("mix_in"), 16 * MIX_LOADS)
                        for tt in range(NT):
                            for k in range(KD):
                                mm(PS[:, b0 + 1, UCOL + FH * tt:UCOL + FH * (tt + 1)], HT[:, k, P * tt:P * (tt + 1)],
                                   WF[:, k, :], start=k == 0, stop=k == KD - 1)
                for k in range(KD):
                    last = mm(PS[:, b0 + t // 2, UCOL * (t % 2):UCOL * (t % 2) + UCOL],
                              HT[:, k, P * t:P * (t + 1)], w[:, k, :], start=k == 0, stop=k == KD - 1)
                if t == NT - 1:
                    last.then_inc(S("proj_done"), 1)

            for u in range(NEAR + 1):
                for t in range(NT):
                    project_in(u, t)
            pe.wait_ge(S("pj_ready"), NEAR)
            pe.wait_ge(S("lf_ready"), 1)
            mm(PS[:, 0, 0:8], C["tri"], LF[:, 0, :], start=True, stop=True)
            mm(PS[:, 0, 8:16], C["tri"], LF[:, 1, :], start=True, stop=False)
            mm(PS[:, 0, 8:16], C["ones"], LF[:, 0, :], start=False, stop=True)
            mm(PS[:, 0, 16:24], C["blk"], LF[:, 2, :], start=True, stop=False)
            for b in range(NS):
                one = C["sel"][:, P - LS - LS * b:2 * P - LS - LS * b]
                mm(PS[:, 0, 16:24], one, CLF[:, b, :], start=False, stop=b == NS - 1)
            mm(PS[0:FH, 1, 0:P], LF[:, 0, :], C["tri"], start=True, stop=True)
            mm(PS[0:FH, 1, P:2 * P], LF[:, 1, :], C["tri"], start=True, stop=False)
            mm(PS[0:FH, 1, P:2 * P], LF[:, 0, :], C["ones"], start=False, stop=True)
            for b in range(NS):
                out = PS[0:FH, 2 + b // 3, KEYS * (b % 3):KEYS * (b % 3) + KEYS]
                mm(out[:, 0:PAST], CLF[:, b, :], C["tri"], start=True, stop=True)
                mm(out[:, PAST:KEYS], CLF[:, b, :], C["ones"][:, 0:LS], start=True, stop=False)
                last = mm(out[:, PAST:KEYS], LF[:, 2, :], C["blk"][:, LS * b:LS * (b + 1)], start=False, stop=True)
            last.then_inc(S("csum_done"), 1)
            project_in(NEAR + 1, 0)
            project_in(NEAR + 1, 1)
            pe.wait_ge(S("q_ready"), 1)
            pe.wait_ge(S("k_ready"), 1)
            pe.wait_ge(S("csum_read"), 4)
            for i in range(2 * FH):
                h, isk = divmod(i, 2)
                if i >= 6:
                    pe.wait_ge(S("kt_ready" if isk else "qt_ready"), h - 2)
                for t in range(NT):
                    c0 = (KO if isk else QO) + FD * h
                    last = nc.tensor.transpose(PS[0:FD, i % 6, P * t:P * (t + 1)], PJ[:, t, c0:c0 + FD], ident)
                last.then_inc(S("qk_tr"), 1)
            pe.wait_ge(S("qt_ready"), FH)
            pe.wait_ge(S("kt_ready"), FH)

            def scores(h):
                if h >= 2:
                    pe.wait_ge(S("scores_masked"), h - 1)
                mm(PS[:, h % 2, 0:P], QT[0:72, h, 0:P], KT[0:72, h, 0:P], start=True, stop=True)
                mm(PS[:, h % 2, P:3 * P], QT[0:72, h, P:2 * P], KT[0:72, h, 0:2 * P], start=True, stop=True
                   ).then_inc(S("scores_done"), 1)

            scores(0)
            for h in range(FH + 1):
                if h + 1 < FH:
                    scores(h + 1)
                if h < FH:
                    pe.wait_ge(S("probs_ready"), h + 1)
                    if h >= 2:
                        pe.wait_ge(S("probsT_ready"), h - 1)
                    for i in range(3):
                        last = nc.tensor.transpose(PS[:, 2 + h % 2, P * i:P * (i + 1)],
                                                   SS[:, h % 2, P * i:P * (i + 1)], ident)
                    last.then_inc(S("probs_tr"), 1)
                if h >= 1:
                    g = h - 1
                    pe.wait_ge(S("probsT_ready"), g + 1)
                    if g >= 2:
                        pe.wait_ge(S("attn_out"), g - 1)
                    v = [PJ[:, t, VO + FD * g:VO + FD * (g + 1)] for t in range(2)]
                    mm(PS[:, 4 + g % 2, 0:FD], PT[:, g % 2, 0:P], v[0], start=True, stop=True)
                    mm(PS[:, 4 + g % 2, FD:2 * FD], PT[:, g % 2, P:2 * P], v[0], start=True, stop=False)
                    mm(PS[:, 4 + g % 2, FD:2 * FD], PT[:, g % 2, 2 * P:3 * P], v[1], start=False, stop=True
                       ).then_inc(S("attn_done"), 1)
                if h == 0:
                    project_in(NEAR + 1, 2)
                project_in(NEAR + 2 + h // NT, h % NT)
            pe.wait_ge(S("attn_out"), FH)
            for b in range(NS):
                n = N_IN + b // 4
                if b % 4 == 0:
                    full("a", n)
                if b >= 2:
                    pe.wait_ge(S("ktc_even" if b % 2 == 0 else "ktc_odd"), b // 2)
                kc = slot[n % LO][:, :].rearrange("p (b c) -> p b c", b=4)
                for h in range(FH):
                    last = nc.tensor.transpose(PS[0:FD, 2 * (b % 2) + h // 4, P * (h % 4):P * (h % 4) + P],
                                               kc[:, b % 4, FD * h:FD * (h + 1)], ident)
                last.then_inc(S("cachek_tr"), 1)
                if b % 2 and b < 2 * NT:
                    project_in(N_IN - 1, b // 2)
            pe.wait_ge(S("ktc_even"), 4)
            pe.wait_ge(S("ktc_odd"), 4)
            pe.wait_ge(S("ktc_new"), 1)
            for h in range(FH):
                if h >= 2:
                    pe.wait_ge(S("s_masked"), h - 1)
                for par in range(2):
                    for j in range(4):
                        last = mm(PS[32 * j:32 * j + 32, 4 + h % 2, KEYS * par:KEYS * (par + 1)],
                                  QT[0:72, h, 2 * P + 32 * j:2 * P + 32 * j + 32], KTC[0:72, 2 * j + par, h, :],
                                  start=True, stop=True, tile_position=(0, 32 * j))
                last.then_inc(S("s_done"), 1)
            pe.wait_ge(S("s_probs"), 1)
            full("a", N_IN + 2)
            full("a", N_IN + 3)

            def sample_out(h):
                pe.wait_ge(S("sT_ready"), h + 1)
                out = PS[:, 2, FD * h:FD * (h + 1)]
                mm(out, PT[:, h % 2, 2 * P:3 * P], PJ[:, 2, VO + FD * h:VO + FD * (h + 1)], start=True, stop=False,
                   skip_group_check=True)
                for par in range(2):
                    for j in range(4):
                        b = 2 * j + par
                        vc = slot[(N_IN + 2 + b // 4) % LO][:, :].rearrange("p (b c) -> p b c", b=4)
                        last = mm(out[32 * j:32 * j + 32, :], PT[:, h % 2, P * par + 32 * j:P * par + 32 * j + 32],
                                  vc[:, b % 4, FD * h:FD * (h + 1)], start=False, stop=par == 1,
                                  skip_group_check=True, tile_position=(0, 32 * j))
                last.then_inc(S("so_done"), 1)

            for h in range(FH + 1):
                if h < FH:
                    if h >= 2:
                        pe.wait_ge(S("sT_ready"), h - 1)
                        pe.wait_ge(S("so_done"), h - 1)
                    for i in range(3):
                        src = PN[:, h, :] if i == 2 else ES[:, 2 * h + i, 0:PAST]
                        last = nc.tensor.transpose(PS[:, h % 2, P * i:P * (i + 1)], src, ident)
                    last.then_inc(S("sT_done"), 1)
                if h >= 1:
                    sample_out(h - 1)

            pe.wait_ge(S("rot_ready"), NT)
            pe.wait_ge(S("fox_done"), 1)
            for i in range(2 * RH):
                for t in range(NT):
                    last = nc.tensor.transpose(PS[0:RK, i, P * t:P * (t + 1)], RT[:, t, i, :], ident)
                last.then_inc(S("ret_tr"), 1)
            pe.wait_ge(S("qrt_even"), 4)
            pe.wait_ge(S("qrt_odd"), 4)

            def ret_scores(h):
                if h >= 2:
                    pe.wait_ge(S("sd_ready"), h - 1)
                for t in range(NT):
                    tt = slice(P * t, P * (t + 1))
                    last = mm(PS[:, h % 2, tt], QRT[0:RK, RH + h, tt], QRT[0:RK, h, tt], start=True, stop=True)
                last.then_inc(S("rs_done"), 1)
                if h >= 2:
                    pe.wait_ge(S("s2_ready"), h - 1)
                for t in range(2):
                    last = mm(PS[0:RK, 4 + h % 2, P * t:P * (t + 1)], KDP[:, t, h, :],
                              PJ[:, t, RVO + RV * h:RVO + RV * (h + 1)], start=True, stop=True)
                last.then_inc(S("sadd_done"), 1)

            ret_scores(0)
            for h in range(RH):
                if h + 1 < RH:
                    ret_scores(h + 1)
                pe.wait_ge(S("qd_ready"), 1)
                pe.wait_ge(S("sd_ready"), h + 1)
                pe.wait_ge(S("s2_ready"), h + 1)
                if h >= 2:
                    pe.wait_ge(S("yr_ready"), NT * (h - 1))
                v = [PJ[:, t, RVO + RV * h:RVO + RV * (h + 1)] for t in range(NT)]
                mm(PS[:, 2 + h % 2, 0:P], SD[:, h % 2, 0:P], v[0], start=True, stop=True)
                mm(PS[:, 2 + h % 2, P:2 * P], SD[:, h % 2, P:2 * P], v[1], start=True, stop=False)
                mm(PS[:, 2 + h % 2, P:2 * P], QD1[0:RK, h, :], S1[0:RK, h, 0, :], start=False, stop=True)
                out = PS[:, 2 + h % 2, 2 * P:3 * P]
                mm(out, SD[:, h % 2, 2 * P:3 * P], v[2], start=True, stop=False, skip_group_check=True)
                for j in range(4):
                    last = mm(out[32 * j:32 * j + 32, :], QD2[:, h, 32 * j:32 * j + 32], STt[:, j, h, :],
                              start=False, stop=True, skip_group_check=True, tile_position=(0, 32 * j))
                last.then_inc(S("y_done"), 1)
            pe.wait_ge(S("vm_ready"), 1)
            for j in range(4):
                if j >= 2:
                    pe.wait_ge(S("stn_ready"), j - 1)
                for h in range(RH):
                    last = mm(PS[:, 6 + j % 2, RV * h:RV * (h + 1)], KDS[:, h, :, :],
                              VM[:, j, RV * h:RV * (h + 1)], start=True, stop=True)
                last.then_inc(S("sstate_done"), 1)

            pe.wait_ge(S("mix_ready"), 1)
            transpose_stream(PJ)
            wait_stream(2)

            def project_out(seg, first, lhs, done, added, parts=None):
                for u in range(4):
                    full(seg, first + u)
                    if u >= 2:
                        pe.wait_ge(S("x_mixed"), added + 2 * (u - 1))
                    w = dense(first + u)
                    for t in range(NT):
                        for k in range(KD):
                            if parts and u == t == 0:
                                pe.wait_ge(S(parts), k + 1)
                            last = mm(PS[:, 2 * (u % 2) + t // 2, UCOL * (t % 2):UCOL * (t % 2) + UCOL],
                                      lhs[:, k, P * t:P * (t + 1)], w[:, k, :], start=k == 0, stop=k == KD - 1)
                    last.then_inc(S(done), 1)

            project_out("a", N_IN + 4, HT, "wout_done", 0)

            def moe(lay, stream, base):
                pe.wait_ge(S("hn_ready"), NT * (2 * lay + 2))
                transpose_stream(NM)
                wait_stream(stream)
                pe.wait_ge(S("router_in"), 64 * (lay + 1))
                for t in range(NT):
                    for k in range(KD):
                        last = mm(PS[:, 0, NR * t:NR * (t + 1)], HM[:, k, P * t:P * (t + 1)], WR[:, k, :],
                                  start=k == 0, stop=k == KD - 1)
                last.then_inc(S("logits_done"), 1)
                pe.wait_ge(S("chosen"), lay + 1)
                for t in range(NT):
                    out = PS[:, 1, NE * t:NE * (t + 1)]
                    for s in range(t):
                        mm(out, C["ones"], SE[:, s, :], start=s == 0, stop=False)
                    mm(out, C["strict"], SE[:, t, :], start=t == 0, stop=True)
                for t in range(NT):
                    last = mm(PS[:, 1, NE * NT:NE * (NT + 1)], C["ones"], SE[:, t, :], start=t == 0, stop=t == NT - 1)
                last.then_inc(S("ranks_done"), 1)

                def gather(half):
                    for kk in range(4):
                        k = 4 * half + kk
                        out = PS[:, kk // 2, 256 * (kk % 2):256 * (kk % 2) + 256]
                        for t in range(NT):
                            for part, x in enumerate((XHI, XLO)):
                                v = x[:, t, :].rearrange("p (q k) -> p k q", k=KD)[:, k, :]
                                last = mm(out, v, G[:, QUAD * t:QUAD * (t + 1), :], start=t + part == 0,
                                          stop=t + part == NT)
                    last.then_inc(S("gathered"), 1)

                def gate_up(pair):
                    for gu in range(2):
                        for k in range(KD):
                            for e in range(2):
                                w = slot[4 * pair + 2 * e + gu][:, :].rearrange("p (k f) -> p k f", k=KD)
                                last = mm(PS[CAP * e:CAP * (e + 1), 2 + pair, FE * gu:FE * (gu + 1)],
                                          XG[:, k, CAP * (2 * pair + e):CAP * (2 * pair + e + 1)], w[:, k, :],
                                          start=k == 0, stop=k == KD - 1, skip_group_check=True)
                    last.then_inc(S("gu_done"), 1)

                def hidden_transposed(pair, g):
                    pe.wait_ge(S("hid_ready"), g * 2 + (pair + 1))
                    for j in range(2):
                        last = nc.tensor.transpose(PS[:, 2 + pair, P * j:P * (j + 1)], HT2[:, pair, P * j:P * (j + 1)],
                                                   ident)
                    last.then_inc(S("hid_tr"), 1)

                def down(pair, g):
                    pe.wait_ge(S("hidT_ready"), g * 2 + (pair + 3))
                    pe.wait_ge(S("yl_ready"), g * 2 + (pair + 2))
                    for e in range(2):
                        pe.wait_ge(S(f"d_full{2 * pair + e}"), (g + 1) * 16)
                    for n in range(2):
                        for j in range(2):
                            for e in range(2):
                                w = slot[8 + 2 * pair + e][:, :].rearrange("p (j n) -> p j n", j=2)
                                last = mm(PS[CAP * e:CAP * (e + 1), 4 + n, :], HID[:, pair, j, e, :],
                                          w[:, j, 512 * n:512 * (n + 1)], start=j == 0, stop=j == 1,
                                          skip_group_check=True)
                    last.then_inc(S("d_done"), 1)

                def first_pair(g):
                    pe.wait_ge(S("xg_ready"), g * 2 + 2)
                    pe.wait_ge(S("hidT_ready"), g * 2 + 1)
                    for e in range(2):
                        pe.wait_ge(S(f"gu_full{e}"), g * 32 + 32)
                    gate_up(0)

                def step(g, more):
                    pe.wait_ge(S("gw_ready"), g + 1)
                    pe.wait_ge(S("x_added"), g * 6 + 6)
                    for pair in range(2):
                        for t in range(NT):
                            last = nc.tensor.transpose(PS[:, 6 + pair, P * t:P * (t + 1)],
                                                       GW[:, QUAD * t + 2 * pair:QUAD * t + 2 * pair + 2, :], ident)
                        last.then_inc(S("gw_tr"), 1)
                    pe.wait_ge(S("hidT_ready"), g * 2 + 2)
                    for e in range(2, 4):
                        pe.wait_ge(S(f"gu_full{e}"), (g + 1) * 32)
                    gate_up(1)
                    hidden_transposed(0, g)
                    if more:
                        pe.wait_ge(S("g_ready"), g + 2)
                        gather(0)
                    down(0, g)
                    hidden_transposed(1, g)
                    if more:
                        pe.wait_ge(S("xg_ready"), g * 2 + 3)
                        gather(1)
                    down(1, g)
                    if more:
                        first_pair(g + 1)
                    pe.wait_ge(S("gt_ready"), g * 4 + 4)
                    pe.wait_ge(S("yl_ready"), g * 2 + 4)
                    for i in range(2 * NT):
                        t, n = divmod(i, 2)
                        pe.wait_ge(S("x_added"), g * 6 + i + 5)
                        for pair in range(2):
                            for part, y in enumerate((YH, YL)):
                                last = mm(PS[:, 6 + i % 2, :], GT[:, pair, P * t:P * (t + 1)],
                                          y[:, pair, 512 * n:512 * (n + 1)], start=pair + part == 0,
                                          stop=pair + part == 2)
                        last.then_inc(S("sum_done"), 1)

                pe.wait_ge(S("steps_known"), lay + 1)
                n = pe.value_load(NW[0:1, lay:lay + 1], min_val=0, max_val=(MAXWIN - 1) * NQ) + NQ
                pe.wait_ge(S("g_ready"), base + 1)
                gather(0)
                pe.wait_ge(S("xg_ready"), base * 2 + 1)
                gather(1)
                first_pair(base)
                with pe.Fori(base, base + n - 1) as s:
                    step(s, True)
                step(base + n - 1, False)
                return n

            steps0 = moe(0, 3, 0)

            pe.wait_ge(S("conv_in"), 16 * 7)
            pe.wait_ge(S("moe_done"), 1)
            nc.tensor.transpose(PS[:, 6, 0:40], SMR[0:40, :], ident[0:40, 0:40])
            for c in range(KD):
                last = nc.tensor.transpose(PS[:, 6, 64 + 32 * c:64 + 32 * c + CONV_W], WDR[0:CONV_W, P * c:P * (c + 1)],
                                           ident[0:CONV_W, 0:CONV_W])
            last.then_inc(S("taps_tr"), 1)
            for c in range(KD):
                bank = 2 * (c % 2) + (c // 2) % 2
                if c >= 4:
                    pe.wait_ge(S("hist_ready"), c - 3)
                for g in range(2):
                    last = nc.tensor.transpose(PS[:, bank, 120 * g:120 * (g + 1)], CC[0:120, g, P * c:P * (c + 1)],
                                               ident[0:120, 0:120])
                last.then_inc(S("hist_tr"), 1)
            pe.wait_ge(S("hist_ready"), KD)
            pe.wait_ge(S("taps_ready"), 2)
            pe.wait_ge(S("hn_ready"), 3 * NT)
            transpose_stream(NC)
            wait_stream(4)
            for c in range(KD):
                m, cc = divmod(c, 2)
                if cc == 0:
                    full("c", 2 * m)
                    full("c", 2 * m + 1)
                if c >= 4:
                    pe.wait_ge(S("u_ready"), c - 3)
                for g in range(2):
                    w = dense(2 * m + g)
                    for k in range(KD):
                        last = mm(PS[:, 2 * (c % 4) + g, 0:TOK], w[:, k, P * cc:P * (cc + 1)], HC[:, k, :],
                                  start=k == 0, stop=k == KD - 1)
                    if g == 1:
                        last.then_inc(S("glu_done"), 1)
            pe.wait_ge(S("uhist_ready"), KD)
            pe.wait_ge(S("unew_ready"), KD)
            for c in range(KD):
                nc.tensor.transpose(PS[0:HIST, c // 4, P * (c % 4):P * (c % 4 + 1)], U[:, c, PBLK - 1, LS:LS + HIST],
                                    ident)
                last = nc.tensor.transpose(PS[:, 2 + c // 4, P * (c % 4):P * (c % 4 + 1)], UN[:, c, :], ident)
            last.then_inc(S("ctok_tr"), 1)
            for c in range(KD):
                pe.wait_ge(S("y_conv"), c + 1)
                last = mm(PS[:, 6, 0:TOK], C["onesd"], YC[:, c, :], start=c == 0, stop=c == KD - 1)
            last.then_inc(S("mean_done"), 1)
            for c in range(KD):
                pe.wait_ge(S("ysq_ready"), c + 1)
                last = mm(PS[:, 7, 0:TOK], C["onesd"], YS[:, c, :], start=c == 0, stop=c == KD - 1)
            last.then_inc(S("var_done"), 1)
            pe.wait_ge(S("ctok_ready"), 2)
            project_out("c", 8, YC, "pw_done", 8, "z_ready")

            moe(1, 5, steps0)

        @block.scalar
        def _(act):
            q = InOrder(act, S("act_step"))
            A = nc.scalar.activation

            def preload(func):
                q.settle()
                q.link(A(stat[:, 13:14], C["eps"], func))

            def norm_stats(n, dst):
                for t in range(NT):
                    if n == 0:
                        act.wait_ge(S(f"x_in{t}"), 16)
                    q.do(A(dst[:, t, :], X[:, t, :], ACT.Square, accum_out=stat[:, t:t + 1]))
                q.settle()
                if n == 0:
                    act.wait_ge(S("cst_in"), 16)
                q.link(A(stat[:, 3:6], stat[:, 0:3], ACT.Sqrt, scale=1.0 / D, bias=C["eps"]), S("rms_ready"))

            def stream_even(n, dst):
                for k in range(0, KD, 2):
                    act.wait_ge(S("tr_done"), KD * n + k + 1)
                    q.do(A(dst[:, k, :], PS[:, k, 0:TOK], ACT.Copy), S("tr_even"))

            norm_stats(0, HN)
            stream_even(0, HT)
            def projected(u):
                act.wait_ge(S("proj_done"), u + 1)
                b0 = 2 * (u % 4) if u < NEAR else 6
                q.do(A(PJ[:, 0:2, UCOL * u:UCOL * (u + 1)], PS[:, b0, :].rearrange("p (t n) -> p t n", t=2), ACT.Copy))
                if u == FF_COL // UCOL - 1:
                    q.do(A(FF[:, :, :], PS[:, b0 + 1, UCOL:UCOL + NT * FH].rearrange("p (t n) -> p t n", t=NT),
                           ACT.Copy))
                q.do(A(PJ[:, 2, UCOL * u:UCOL * (u + 1)], PS[:, b0 + 1, 0:UCOL], ACT.Copy), S("pj_ready"))

            for u in range(NEAR):
                projected(u)
                if u == 3:
                    act.wait_ge(S("qk_sumsq"), 1)
                    q.link(A(MS[:, :], MS[:, :], ACT.Sqrt, scale=1.0 / FD, bias=C["eps"]), S("qk_rms"))
                if u == 5:
                    act.wait_ge(S("qk_sumsq"), 2)
                    q.link(A(MS[:, :], MS[:, :], ACT.Sqrt, scale=1.0 / FD, bias=C["eps"]), S("qk_rms"))
            act.wait_ge(S("ff_abs"), 1)
            q.link(A(LT[:, :, :], LT[:, :, :], ACT.Exp, scale=-1.0))
            q.link(A(LT[:, :, :], LT[:, :, :], ACT.Ln, bias=1.0), S("ff_ln"))
            projected(NEAR)
            act.wait_ge(S("csum_done"), 1)
            q.do(A(CQ[:, :, :], PS[:, 0, 0:NT * FH].rearrange("p (t h) -> p t h", t=NT), ACT.Copy))
            q.do(A(KT[FD:FD + FH, :, 0:SEQ], bc(PS[0:FH, 1, 0:SEQ], 1, FH), ACT.Copy, scale=-1.0))
            for g in range(3):
                nb = 3 if g < 2 else 2
                for b in range(3 * g, 3 * g + nb):
                    ins = A(KTC[FD:FD + FH, b, :, :], bc(PS[0:FH, 2 + g, KEYS * (b % 3):KEYS * (b % 3 + 1)], 1, FH),
                            ACT.Copy, scale=-1.0)
                    q.do(ins, S("csum_read") if b in (2, 5, 6, 7) else None)
            for h in range(FH):
                act.wait_ge(S("qk_tr"), 2 * h + 1)
                q.do(A(QT[0:FD, h, :], PS[0:FD, (2 * h) % 6, 0:TOK], ACT.Copy), S("qt_ready"))
            def exps(h):
                act.wait_ge(S("scores_masked"), h + 1)
                q.do(A(SS[:, h % 2, 0:P], SS[:, h % 2, 0:P], ACT.Exp, bias=MX[:, 2 * (h % 2):2 * (h % 2) + 1],
                       accum_out=SM[:, 2 * (h % 2):2 * (h % 2) + 1]))
                q.do(A(SS[:, h % 2, P:3 * P], SS[:, h % 2, P:3 * P], ACT.Exp,
                       bias=MX[:, 2 * (h % 2) + 1:2 * (h % 2) + 2],
                       accum_out=SM[:, 2 * (h % 2) + 1:2 * (h % 2) + 2]), S("probs_ready"))

            exps(0)
            for h in range(FH):
                if h + 1 < FH:
                    if h >= 1:
                        act.wait_ge(S("attn_out"), h)
                    exps(h + 1)
                act.wait_ge(S("probs_tr"), h + 1)
                if h >= 2:
                    act.wait_ge(S("attn_done"), h - 1)
                q.do(A(PT[:, h % 2, :], PS[:, 2 + h % 2, 0:TOK], ACT.Copy), S("probsT_ready"))
                if h == 0:
                    projected(NEAR + 1)
                if h % NT == NT - 1:
                    projected(NEAR + 2 + h // NT)
            projected(N_IN - 2)
            for b in range(0, NS, 2):
                act.wait_ge(S("cachek_tr"), b + 1)
                q.do(A(KTC[0:FD, b, :, 0:PAST], PS[0:FD, 0:2, :].rearrange("p a (h n) -> p (a h) n", n=PAST),
                       ACT.Copy), S("ktc_even"))
            projected(N_IN - 1)
            q.settle()
            for i in range(2 * FH):
                if i % FH == 0:
                    act.wait_ge(S("s_max"), i // FH + 1)
                q.do(A(ES[:, i, :], ES[:, i, :], ACT.Exp, bias=MX[:, i:i + 1], accum_out=SM[:, i:i + 1]),
                     S("s_exp"))
            for h in range(0, FH, 2):
                act.wait_ge(S("sT_done"), h + 1)
                if h >= 2:
                    act.wait_ge(S("so_done"), h - 1)
                q.do(A(PT[:, 0, :], PS[:, 0, 0:TOK], ACT.Copy), S("sT_even"))
            act.wait_ge(S("fox_done"), 1)
            act.wait_ge(S("vm_zero"), 1)
            for j in range(4):
                q.do(A(VM[32 * j:32 * j + 32, j, :], PJ[32 * j:32 * j + 32, 2, RVO:RGO], ACT.Copy),
                     S("vm_ready") if j == 3 else None)
            q.do(A(PJ[:, :, RGO:MIX], PJ[:, :, RGO:MIX], ACT.Silu), S("rg_silu"))
            preload(ACT.Sqrt)
            for i in range(0, 2 * RH, 2):
                act.wait_ge(S("ret_tr"), i + 1)
                q.do(A(QRT[0:RK, i, :], PS[0:RK, i, 0:TOK], ACT.Copy), S("qrt_even"))
            act.wait_ge(S("qrt_odd"), 2)
            q.settle()
            q.do(A(QD2[0:RK, :, :], QRT[0:RK, 0:RH, SEQ:TOK], ACT.Copy))
            q.do(A(QD2[RK:P, :, :], QRT[0:RK, 0:RH, SEQ:TOK], ACT.Copy), S("qd2_in"))
            for h in range(RH):
                act.wait_ge(S("y_done"), h + 1)
                for t in range(NT):
                    q.do(A(YR[:, t, h, :], PS[:, 2 + h % 2, P * t:P * (t + 1)], ACT.Copy,
                           accum_out=stat[:, RH * t + h:RH * t + h + 1]), S("yr_ready"))
            for h in range(RH):
                act.wait_ge(S("yr_centred"), h + 1)
                for t in range(NT):
                    q.do(A(YQ[:, t, h, :], YR[:, t, h, :], ACT.Square, accum_out=SM[:, RH * t + h:RH * t + h + 1]))
            q.settle()
            q.link(A(SM[:, 0:12], SM[:, 0:12], ACT.Sqrt, scale=1.0 / RV, bias=C["eps"]), S("yr_rms"))
            stream_even(1, HT)

            def moe(lay, stream, base):
                preload(ACT.Sqrt)
                act.wait_ge(S("x_mixed"), 8 * (lay + 1))
                act.wait_ge(S("stored"), 16 * (STATE_STORES + lay * CONV_STORES))
                norm_stats(2 * lay + 1, NM)
                stream_even(stream - 1, HM)
                preload(ACT.Exp)
                act.wait_ge(S("gl_centred"), lay + 1)
                q.link(A(E4[:, :, :], E4[:, :, :], ACT.Exp), S("gl_exp"))
                act.wait_ge(S("d_ready"), lay + 1)
                q.link(A(R8[:, 21:24], R8[:, 18:21], ACT.Exp), S("d_exp"))
                preload(ACT.Silu)

                def xg(half):
                    q2 = A(XG[:, 4 * half:4 * half + 4, :].rearrange("p k n -> p (k n)"),
                           PS[:, 0:2, :].rearrange("p a n -> p (a n)"), ACT.Copy)
                    q2.then_inc(S("xg_ready"), 1)

                def step(s, more):
                    def hidden_out(pair):
                        act.wait_ge(S("hid_tr"), s * 2 + (pair + 1))
                        A(HID[:, pair, :, :, :].rearrange("p j e n -> p (j e n)"), PS[:, 2 + pair, 0:FE], ACT.Copy
                          ).then_inc(S("hidT_ready"), 1)

                    for pair in range(2):
                        act.wait_ge(S("gu_done"), s * 2 + (pair + 1))
                        A(SG[:, pair, :], PS[:, 2 + pair, 0:FE], ACT.Silu).then_inc(S("silu_ready"), 1)
                    hidden_out(0)
                    for pair in range(2):
                        if pair == 0 and more:
                            act.wait_ge(S("gathered"), s * 2 + 3)
                            xg(0)
                        act.wait_ge(S("d_done"), s * 2 + (pair + 1))
                        act.wait_ge(S("gt_ready"), s * 4 + (2 * pair + 2))
                        A(YH[:, pair, :], PS[:, 4:6, :].rearrange("p a n -> p (a n)"), ACT.Copy,
                          scale=GATE[:, pair:pair + 1]).then_inc(S("yh_ready"), 1)
                        if pair == 0:
                            hidden_out(1)
                            if more:
                                act.wait_ge(S("gathered"), s * 2 + 4)
                                xg(1)

                act.wait_ge(S("steps_known"), lay + 1)
                n = act.value_load(NW[0:1, lay:lay + 1], min_val=0, max_val=(MAXWIN - 1) * NQ) + NQ
                for half in range(2):
                    act.wait_ge(S("gathered"), base * 2 + (half + 1))
                    xg(half)
                with act.Fori(base, base + n - 1) as s:
                    step(s, True)
                step(base + n - 1, False)
                return n

            steps0 = moe(0, 3, 0)
            preload(ACT.Sqrt)
            act.wait_ge(S("moe_done"), 1)
            norm_stats(2, NC)
            act.wait_ge(S("taps_tr"), 1)
            q.do(A(SMT[:, :], PS[:, 6, 0:40], ACT.Copy), S("taps_ready"))
            q.do(A(WDT[:, :, :], PS[:, 6, 64:64 + 32 * KD].rearrange("p (c w) -> p c w", c=KD)[:, :, 0:CONV_W],
                   ACT.Copy), S("taps_ready"))
            for c in range(KD):
                act.wait_ge(S("hist_tr"), c + 1)
                q.do(A(U[:, c, PBLK:, 0:HIST], PS[:, 2 * (c % 2) + (c // 2) % 2, 0:240].rearrange("p (b w) -> p b w", b=NS), ACT.Copy),
                     S("hist_ready"))
            stream_even(3, HC)
            q.settle()

            def sigmoids(c):
                act.wait_ge(S("glu_done"), c + 1)
                if c >= 2:
                    act.wait_ge(S("u_ready"), c - 1)
                q.do(A(SGC[:, c % 2, :], PS[:, 2 * (c % 4) + 1, 0:TOK], ACT.Sigmoid, bias=SMT[:, 8 + c:9 + c]),
                     S("sig_ready"))

            act.wait_ge(S("hist_tr"), KD)
            sigmoids(0)
            for c in range(KD):
                act.wait_ge(S("u_ready"), c + 1)
                q.do(A(U[:, c, 1:PBLK, HIST - LS:HIST], U[:, c, 0:PBLK - 1, HIST:], ACT.Copy))
                q.do(A(U[:, c, 2:PBLK, 0:HIST - LS], U[:, c, 0:PBLK - 2, 2 * LS:], ACT.Copy), S("uhist_ready"))
                q.do(A(UN[:, c, :].rearrange("p (b l) -> p b l", b=NS), U[:, c, PBLK:, HIST:], ACT.Copy),
                     S("unew_ready"))
                q.settle()
                if c + 1 < KD:
                    sigmoids(c + 1)
                if c >= 2:
                    act.wait_ge(S("y_conv"), c - 1)
                for w in range(POOL_TAPS):
                    n = c * (POOL_TAPS - 1) + w
                    if w and n > 2:
                        act.wait_ge(S("pool_tap"), n - 2)
                    dst = (PR[:, (n - 1) % 2, :] if w else YP[:, c % 2, :]).rearrange("p (b l) -> p b l", l=LS)
                    q.do(A(dst, U[:, c, :, w:w + LS], ACT.Copy, scale=WDT[:, c, w:w + 1]),
                         S("product_ready" if w else "first_product"))
            act.wait_ge(S("ctok_tr"), 1)
            q.do(A(CP[0:HIST, :], PS[0:HIST, 0:2, :].rearrange("p a n -> p (a n)"), ACT.Copy), S("ctok_ready"))
            q.do(A(CS[:, :], PS[:, 2:4, :].rearrange("p a n -> p (a n)"), ACT.Copy), S("ctok_ready"))
            preload(ACT.Sqrt)
            for c in range(KD):
                act.wait_ge(S("yc_centred"), c + 1)
                q.do(A(YS[:, c, :], YC[:, c, :], ACT.Square), S("ysq_ready"))
            act.wait_ge(S("var_done"), 1)
            q.link(A(VR[:, :], PS[:, 7, 0:TOK], ACT.Sqrt, bias=C["eps"]), S("cstd_ready"))
            preload(ACT.Silu)
            for c in range(KD):
                act.wait_ge(S("yc_normed"), c + 1)
                q.do(A(YC[:, c, :], YC[:, c, :], ACT.Silu, scale=SMT[:, 24 + c:25 + c], bias=SMT[:, 32 + c:33 + c]),
                     S("z_ready"))
            moe(1, 5, steps0)

        @block.vector
        def _(dve):
            q = InOrder(dve, S("dve_step"))
            V = nc.vector

            def tt(out, in0, in1, op, sem=None):
                q.link(V.tensor_tensor(out, in0, in1, op), sem)

            def ts(out, in0, s1, s2, op0, op1=None, sem=None):
                if op1 is None:
                    q.link(V.tensor_scalar(out, in0, s1, None, op0), sem)
                else:
                    q.link(V.tensor_scalar(out, in0, s1, s2, op0, op1), sem)

            def red(out, in_, op, sem=None, negate=None):
                q.link(V.tensor_reduce(out=out, in_=in_, axis=AXX, op=op, negate=negate), sem)

            def norm_apply(n, dst):
                dve.wait_ge(S("rms_ready"), n + 1)
                if n:
                    dve.wait_ge(S("gain_in"), 16 * n)
                else:
                    dve.wait_ge(S("gain0_in"), 16)
                q.link(V.reciprocal(stat[:, 6:9], stat[:, 3:6]))
                for t in range(NT):
                    q.do(V.scalar_tensor_tensor(dst[:, t, :], X[:, t, :], stat[:, 6 + t:7 + t], gb[:, :], ALU.mult,
                                                ALU.mult), S("hn_ready"))
                q.settle()

            def stream_odd(n, dst):
                for k in range(1, KD, 2):
                    dve.wait_ge(S("tr_done"), KD * n + k + 1)
                    q.do(V.tensor_copy(dst[:, k, :], PS[:, k, 0:TOK]), S("tr_odd"))
                q.settle()

            norm_apply(0, HN)
            stream_odd(0, HT)
            for i, (c0, gain) in enumerate(((QO, GQ), (KO, GK))):
                dve.wait_ge(S("pj_ready"), 2 * i + 2)
                if i == 0:
                    dve.wait_ge(S("mix_in"), 16 * MIX_LOADS)
                    ts(GQ[:, :], GQ[:, :], FD ** -0.5, None, ALU.mult)
                src = PJ[:, :, c0:c0 + FH * FD]
                tt(SQ[:, :, :], src, src, ALU.mult)
                red(MS[:, :].rearrange("p (t h) -> p t h", t=NT), SQ[:, :, :].rearrange("p t (h d) -> p t h d", d=FD),
                    ALU.add, S("qk_sumsq"))
                dve.wait_ge(S("qk_rms"), i + 1)
                q.link(V.reciprocal(MS[:, :], MS[:, :]))
                for t in range(NT):
                    v = PJ[:, t, c0:c0 + FH * FD].rearrange("p (h d) -> p h d", d=FD)
                    tt(v, v, bc(MS[:, FH * t:FH * (t + 1)], 2, FD), ALU.mult)
                    tt(v, v, bc(gain[:, :], 1, FH), ALU.mult, S("q_ready" if i == 0 else "k_ready") if t == 2 else None)
            dve.wait_ge(S("pj_ready"), 6)
            tt(FF[:, :, :], FF[:, :, :], bc(BF[:, :], 1, NT), ALU.add)
            lt, ff = (v[:, :, :].rearrange("p t h -> p (t h)") for v in (LT, FF))
            q.link(V.scalar_tensor_tensor(lt, ff, -1.0, ff, ALU.mult, ALU.max), S("ff_abs"))
            ts(FF[:, :, :], FF[:, :, :], 0.0, None, ALU.min)
            dve.wait_ge(S("ff_ln"), 1)
            tt(LF[:, :, :], FF[:, :, :], LT[:, :, :], ALU.subtract, S("lf_ready"))
            for h in range(FH):
                dve.wait_ge(S("qk_tr"), 2 * h + 2)
                q.do(V.tensor_copy(KT[0:FD, h, :], PS[0:FD, (2 * h + 1) % 6, 0:TOK]), S("kt_ready"))
            q.settle()

            def mask(h):
                dve.wait_ge(S("scores_done"), h + 1)
                if h >= 2:
                    dve.wait_ge(S("probs_tr"), h - 1)
                m = 2 * (h % 2)
                q.do(V.scalar_tensor_tensor(SS[:, h % 2, 0:P], PS[:, h % 2, 0:P], CQ[:, 0, h:h + 1],
                                            C["mask"][:, P:2 * P], ALU.add, ALU.add))
                q.link(V.scalar_tensor_tensor(SS[:, h % 2, P:3 * P], PS[:, h % 2, P:3 * P], CQ[:, 1, h:h + 1],
                                              C["mask"], ALU.add, ALU.add))
                q.do(V.tensor_reduce(out=MX[:, m:m + 1], in_=SS[:, h % 2, 0:P], axis=AXX, op=ALU.max, negate=True))
                q.link(V.tensor_reduce(out=MX[:, m + 1:m + 2], in_=SS[:, h % 2, P:3 * P], axis=AXX, op=ALU.max,
                                       negate=True), S("scores_masked"))

            dve.wait_ge(S("csum_read"), 4)
            mask(0)
            for h in range(FH + 1):
                if h + 1 < FH:
                    mask(h + 1)
                if h >= 1:
                    g = h - 1
                    dve.wait_ge(S("attn_done"), g + 1)
                    m = 2 * (g % 2)
                    q.link(V.reciprocal(RR[:, m:m + 2], SM[:, m:m + 2]))
                    for t in range(2):
                        q.do(V.tensor_scalar(PJ[:, t, QO + FD * g:QO + FD * (g + 1)], PS[:, 4 + g % 2, FD * t:FD * (t + 1)],
                                             RR[:, m + t:m + t + 1], None, ALU.mult),
                             S("attn_out") if t else None)
                    q.settle()
            q.do(V.tensor_copy(KTC[0:FD, :, :, PAST:KEYS],
                               KT[0:FD, :, SEQ:TOK].rearrange("p h (b l) -> p b h l", l=LS)), S("ktc_new"))
            for b in range(1, NS, 2):
                dve.wait_ge(S("cachek_tr"), b + 1)
                q.do(V.tensor_copy(KTC[0:FD, b, :, 0:PAST], PS[0:FD, 2:4, :].rearrange("p a (h n) -> p (a h) n", n=PAST)),
                     S("ktc_odd"))
            q.settle()
            for h in range(FH):
                dve.wait_ge(S("s_done"), h + 1)
                q.do(V.scalar_tensor_tensor(ES[:, 2 * h:2 * h + 2, :],
                                            PS[:, 4 + h % 2, 0:2 * KEYS].rearrange("p (a n) -> p a n", a=2),
                                            CQ[:, 2, h:h + 1], bc(C["smask"], 1, 2), ALU.add, ALU.add), S("s_masked"))
                if h % 4 == 3:
                    q.settle()
                    half = slice(2 * (h - 3), 2 * (h + 1))
                    red(MX[:, half], ES[:, half, :], ALU.max, S("s_max"), negate=True)
            dve.wait_ge(S("s_done"), FH)
            q.link(V.memset(PN[:, :, :], 0.0))
            dve.wait_ge(S("s_exp"), 2 * FH)
            q.link(V.reciprocal(RR[:, 0:16], SM[:, 0:16]))
            tt(RR[:, 0:16].rearrange("p (h a) -> p h a", a=2), RR[:, 0:16].rearrange("p (h a) -> p h a", a=2),
               bc(C["rowpar"], 1, FH), ALU.mult)
            tt(ES[:, :, :], ES[:, :, :], bc(RR[:, 0:16], 2, KEYS), ALU.mult)
            for j in range(4):
                q.do(V.tensor_copy(PN[32 * j:32 * j + 32, :, 32 * j:32 * j + 32].rearrange("p h (a l) -> p h a l", a=2),
                                   ES[32 * j:32 * j + 32, :, PAST:KEYS].rearrange("p (h a) l -> p h a l", a=2)),
                     S("s_probs") if j == 3 else None)
            q.settle()
            x1 = PJ[:, :, RQO:RVO].rearrange("p t (g h d) -> p t g h d", h=2, d=RK // 2)

            def rotate(t):
                cos = bc(C["cos"][:, 32 * t:32 * (t + 1)], 1, 2 * RH)
                sin = bc(C["sin"][:, 32 * t:32 * (t + 1)], 1, 2 * RH)
                lo, hi = x1[:, t, :, 0, :], x1[:, t, :, 1, :]
                q.do(V.tensor_tensor(T1[:, t], lo, cos, ALU.mult))
                q.link(V.tensor_tensor(T2[:, t], hi, sin, ALU.mult))
                q.link(V.tensor_tensor(RT[:, t, :, 0:RK // 2], T1[:, t], T2[:, t], ALU.subtract))
                q.do(V.tensor_tensor(T1[:, t], lo, sin, ALU.mult))
                q.link(V.tensor_tensor(T2[:, t], hi, cos, ALU.mult))
                q.link(V.tensor_tensor(RT[:, t, :, RK // 2:RK], T1[:, t], T2[:, t], ALU.add))
                ts(RT[:, t, RH:2 * RH, :], RT[:, t, RH:2 * RH, :], RK ** -0.5, None, ALU.mult, sem=S("rot_ready"))

            dve.wait_ge(S("pj_ready"), N_IN)
            for h in range(FH):
                dve.wait_ge(S("sT_done"), h + 1)
                if h % 2 == 0:
                    dve.wait_ge(S("sT_even"), h // 2 + 1)
                    q.link(V.tensor_copy(stat[:, 15:16], C["eps"]), S("sT_ready"))
                else:
                    if h >= 2:
                        dve.wait_ge(S("so_done"), h - 1)
                    q.link(V.tensor_copy(PT[:, 1, :], PS[:, 1, 0:TOK]), S("sT_ready"))
                    if h // 2 < NT:
                        rotate(h // 2)
            dve.wait_ge(S("so_done"), FH)
            q.link(V.tensor_copy(PJ[:, 2, QO:KO], PS[:, 2, :]), S("fox_done"))
            dve.wait_ge(S("ret_in"), 32)
            for t in range(2):
                tt(KDP[:, t], RT[:, t, RH:2 * RH, :], bc(RC["kdec_p"], 2, RK), ALU.mult)
            for par in range(2):
                tt(KDS[:, :, par, :], RT[:, 2, RH:2 * RH, :],
                   bc(RC["kdec_s"].rearrange("p (h a) -> p h a", a=2)[:, :, par], 2, RK), ALU.mult)
            for i in range(1, 2 * RH, 2):
                dve.wait_ge(S("ret_tr"), i + 1)
                q.do(V.tensor_copy(QRT[0:RK, i, :], PS[0:RK, i, 0:TOK]), S("qrt_odd"))
            q.settle()
            dve.wait_ge(S("qrt_even"), 4)
            tt(QD1[0:RK], QRT[0:RK, 0:RH, P:2 * P], RC["qdec_p"][0:RK].rearrange("p (h n) -> p h n", h=RH), ALU.mult)
            dve.wait_ge(S("qd2_in"), 1)
            tt(QD2[:, :, :], QD2[:, :, :], RC["qdec_s"].rearrange("p (h n) -> p h n", h=RH), ALU.mult, S("qd_ready"))
            gam = gammas()

            def decay(h):
                dve.wait_ge(S("rs_done"), h + 1)
                if h >= 2:
                    dve.wait_ge(S("y_done"), h - 1)
                q.do(V.tensor_tensor(SD[:, h % 2, 0:SEQ].rearrange("p (t n) -> p t n", t=2),
                                     PS[:, h % 2, 0:SEQ].rearrange("p (t n) -> p t n", t=2),
                                     bc(RC["dec_p"][:, P * h:P * (h + 1)], 1, 2), ALU.mult))
                q.do(V.tensor_tensor(SD[:, h % 2, SEQ:TOK], PS[:, h % 2, SEQ:TOK], RC["dec_s"][:, P * h:P * (h + 1)],
                                     ALU.mult), S("sd_ready"))
                dve.wait_ge(S("sadd_done"), h + 1)
                q.link(V.tensor_copy(S1[0:RK, h, 0, :], PS[0:RK, 4 + h % 2, 0:P]))
                q.link(V.scalar_tensor_tensor(S1[0:RK, h, 1, :], S1[0:RK, h, 0, :], float(gam[h] ** P),
                                              PS[0:RK, 4 + h % 2, P:2 * P], ALU.mult, ALU.add), S("s2_ready"))

            def centre(h):
                dve.wait_ge(S("yr_ready"), NT * (h + 1))
                mean = stat[:, 0:12].rearrange("p (t h) -> p t h", h=RH)[:, :, h]
                ts(mean, mean, 1.0 / RV, None, ALU.mult)
                tt(YR[:, :, h, :], YR[:, :, h, :], bc(mean, 2, RV), ALU.subtract, S("yr_centred"))

            for h in range(RH):
                decay(h)
                if h >= 2:
                    centre(h - 2)
            dve.wait_ge(S("rg_silu"), 1)
            tt(PJ[:, :, RGO:MIX], PJ[:, :, RGO:MIX], bc(GN[:, :], 1, NT), ALU.mult)
            centre(RH - 2)
            centre(RH - 1)
            for j in range(4):
                dve.wait_ge(S("sstate_done"), j + 1)
                for h in range(RH):
                    q.do(V.scalar_tensor_tensor(STN[:, j, h, :], STt[:, j, h, :], float(gam[h] ** LS),
                                                PS[:, 6 + j % 2, RV * h:RV * (h + 1)], ALU.mult, ALU.add),
                         S("stn_ready") if h == RH - 1 else None)
            q.settle()
            yr = YR[:, :, :, :].rearrange("p t h v -> p (t h) v")
            dve.wait_ge(S("yr_rms"), 1)
            q.link(V.reciprocal(SM[:, 0:12], SM[:, 0:12]))
            tt(yr, yr, bc(SM[:, 0:12], 2, RV), ALU.mult)
            yt = YR[:, :, :, :].rearrange("p t h v -> p t (h v)")
            dve.wait_ge(S("k_stored"), 32)
            tt(PJ[:, :, KO:VO], yt, PJ[:, :, RGO:MIX], ALU.mult, S("mix_ready"))
            stream_odd(1, HT)

            def add_projection(done, base_):
                for u in range(4):
                    dve.wait_ge(S(done), base_ + u + 1)
                    b0 = 2 * (u % 2)
                    xa, xb = X[:, 0:2, UCOL * u:UCOL * (u + 1)], X[:, 2, UCOL * u:UCOL * (u + 1)]
                    q.do(V.tensor_tensor(xa, xa, PS[:, b0, :].rearrange("p (t n) -> p t n", t=2), ALU.add), S("x_mixed"))
                    q.do(V.tensor_tensor(xb, xb, PS[:, b0 + 1, 0:UCOL], ALU.add), S("x_mixed"))
                q.settle()

            add_projection("wout_done", 0)

            def first_max(onehot, vals, best, rank_, tie):
                red(best, vals, ALU.max)
                tt(onehot, vals, bc(best, 2, vals.shape[2]), ALU.is_equal)
                if len(tie.shape) == 2:
                    tie = bc(tie, 1, NT)
                    tt(onehot, onehot, tie, ALU.mult)
                else:
                    for t in range(NT):
                        v = onehot[:, t, :].rearrange("p (g e) -> p g e", g=NG)
                        q.do(V.tensor_tensor(v, v, tie, ALU.mult))
                    q.settle()
                red(rank_, onehot, ALU.max)
                tt(onehot, onehot, bc(rank_, 2, vals.shape[2]), ALU.is_equal)

            def moe(lay, stream, base):
                norm_apply(2 * lay + 1, NM)
                stream_odd(stream - 1, HM)
                q.link(V.tensor_copy(XHI[:, :, :], NM[:, :, :]))
                tt(XLO[:, :, :], NM[:, :, :], XHI[:, :, :].bitcast(F32), ALU.subtract)
                dve.wait_ge(S("router_in"), 64 * (lay + 1))
                dve.wait_ge(S("logits_done"), lay + 1)
                tt(LG[:, :, :], PS[:, 0, 0:NT * NR].rearrange("p (t n) -> p t n", t=NT), bc(BR[:, :], 1, NT), ALU.add)
                gl = LG[:, :, 0:NG]
                first_max(OH[:, :, :], gl, R8[:, 0:3], R8[:, 3:6], C["tie"][:, 0:NG])
                tt(E4[:, :, :], gl, bc(R8[:, 0:3], 2, NG), ALU.subtract, S("gl_centred"))
                for t in range(NT):
                    q.do(V.tensor_tensor(SE[:, t, :].rearrange("p (g e) -> p g e", g=NG),
                                         LG[:, t, NG:NR].rearrange("p (g e) -> p g e", g=NG),
                                         bc(OH[:, t, :], 2, EPG), ALU.mult))
                ts(FAR[:, :, :], OH[:, :, :], -NEG, NEG, ALU.mult, ALU.add)
                for t in range(NT):
                    v = SE[:, t, :].rearrange("p (g e) -> p g e", g=NG)
                    q.do(V.tensor_tensor(v, v, bc(FAR[:, t, :], 2, EPG), ALU.add))
                q.settle()
                tie = bc(C["tie"], 1, NG)
                first_max(O1[:, :, :], SE[:, :, :], R8[:, 12:15], R8[:, 3:6], tie)
                q.link(V.scalar_tensor_tensor(SE[:, :, :], O1[:, :, :], 2 * NEG, SE[:, :, :], ALU.mult, ALU.add))
                first_max(O2[:, :, :], SE[:, :, :], R8[:, 15:18], R8[:, 3:6], tie)
                tt(SE[:, :, :], O1[:, :, :], O2[:, :, :], ALU.add, S("chosen"))
                tt(R8[:, 18:21], R8[:, 15:18], R8[:, 12:15], ALU.subtract, S("d_ready"))
                dve.wait_ge(S("gl_exp"), lay + 1)
                red(R8[:, 6:9], E4[:, :, :], ALU.add)
                q.link(V.reciprocal(R8[:, 9:12], R8[:, 6:9]))
                dve.wait_ge(S("d_exp"), lay + 1)
                ts(R8[:, 24:27], R8[:, 21:24], 1.0, None, ALU.add)
                q.link(V.reciprocal(R8[:, 24:27], R8[:, 24:27]))
                tt(R8[:, 27:30], R8[:, 24:27], R8[:, 9:12], ALU.mult)
                tt(R8[:, 30:33], R8[:, 27:30], R8[:, 21:24], ALU.mult)
                tt(O1[:, :, :], O1[:, :, :], bc(R8[:, 27:30], 2, NE), ALU.mult)
                tt(O2[:, :, :], O2[:, :, :], bc(R8[:, 30:33], 2, NE), ALU.mult)
                tt(WG[:, :, :], O1[:, :, :], O2[:, :, :], ALU.add)
                wg = WG[:, :, :].rearrange("p t (q e) -> p q t e", e=QUAD)
                for w in range(MAXWIN):
                    dst = WV[:, NQ * w:NQ * (w + 1), :].rearrange("p q (t e) -> p q t e", e=QUAD)
                    q.do(V.tensor_copy(dst, wg))
                dve.wait_ge(S("ranks_done"), lay + 1)
                ts(SL[:, :, :], PS[:, 1, 0:NT * NE].rearrange("p (t n) -> p t n", t=NT), 1.0, None, ALU.add)
                q.link(V.tensor_reduce(out=R8[:, 33:34], in_=PS[:, 1, NT * NE:(NT + 1) * NE], axis=AXX, op=ALU.max))
                tt(SL[:, :, :], SL[:, :, :], SE[:, :, :], ALU.mult)
                sl = SL[:, :, :].rearrange("p t (q e) -> p q t e", e=QUAD)
                for w in range(MAXWIN):
                    dst = SV[:, NQ * w:NQ * (w + 1), :].rearrange("p q (t e) -> p q t e", e=QUAD)
                    q.do(V.tensor_scalar(dst, sl, -1.0 - CAP * w, None, ALU.add))
                q.settle()
                ts(R8[:, 34:39], C["iota"][:, 1:MAXWIN], float(CAP), None, ALU.mult)
                ts(R8[:, 34:39], R8[:, 34:39], R8[:, 33:34], None, ALU.is_lt)
                red(R8[:, 39:40], R8[:, 34:39], ALU.add)
                ts(NW[:, lay:lay + 1], R8[:, 39:40], float(NQ), None, ALU.mult, sem=S("steps_known"))
                n = dve.value_load(NW[0:1, lay:lay + 1], min_val=0, max_val=(MAXWIN - 1) * NQ) + NQ
                if lay == 0:
                    dve.sem_inc(S("hidT_ready"), 2)
                    dve.sem_inc(S("yl_ready"), 2)
                    dve.sem_inc(S("x_added"), 6)

                def onehot(s):
                    V.tensor_tensor(G[:, :, :], bc(C["iota"], 1, NT * QUAD),
                                    bc(SV[:, bass.ds(s, 1), :].rearrange("p o n -> p (o n)"), 2, CAP),
                                    ALU.is_equal).then_inc(S("g_ready"), 1)

                def weighted(s):
                    dve.wait_ge(S("g_ready"), base + s + 1)
                    V.tensor_tensor(GW[:, :, :], G[:, :, :].bitcast(F32),
                                    bc(WV[:, bass.ds(s, 1), :].rearrange("p o n -> p (o n)"), 2, CAP),
                                    ALU.mult).then_inc(S("gw_ready"), 1)

                def step(s, more):
                    g = base + s

                    def hidden(pair):
                        dve.wait_ge(S("silu_ready"), g * 2 + (pair + 1))
                        V.tensor_tensor(HT2[:, pair, :], PS[:, 2 + pair, FE:2 * FE], SG[:, pair, :],
                                        ALU.mult).then_inc(S("hid_ready"), 1)

                    hidden(0)
                    if more:
                        dve.wait_ge(S("gathered"), g * 2 + 2)
                        dve.wait_ge(S("gw_ready"), g + 1)
                        onehot(s + 1)
                    for pair in range(2):
                        dve.wait_ge(S("gw_tr"), g * 2 + (pair + 1))
                        V.tensor_scalar(GT[:, pair, :], PS[:, 6 + pair, 0:TOK], 0.0, None,
                                        ALU.is_gt).then_inc(S("gt_ready"), 1)
                        V.tensor_reduce(out=GATE[:, pair:pair + 1], in_=PS[:, 6 + pair, 0:TOK], axis=AXX,
                                        op=ALU.add).then_inc(S("gt_ready"), 1)
                    hidden(1)
                    if more:
                        weighted(s + 1)
                    for pair in range(2):
                        dve.wait_ge(S("yh_ready"), g * 2 + (pair + 1))
                        dve.wait_ge(S("gt_ready"), g * 4 + (2 * pair + 2))
                        V.scalar_tensor_tensor(YL[:, pair, :], PS[:, 4:6, :].rearrange("p a n -> p (a n)"),
                                               GATE[:, pair:pair + 1], YH[:, pair, :].bitcast(F32), ALU.mult,
                                               ALU.subtract).then_inc(S("yl_ready"), 1)
                    for i in range(2 * NT):
                        t, h = divmod(i, 2)
                        dve.wait_ge(S("sum_done"), g * 6 + (i + 1))
                        v = X[:, t, 512 * h:512 * (h + 1)]
                        V.tensor_tensor(v, v, PS[:, 6 + i % 2, :], ALU.add).then_inc(S("x_added"), 1)

                dve.wait_ge(S("steps_known"), lay + 1)
                onehot(0)
                weighted(0)
                with dve.Fori(0, n - 1) as s:
                    step(s, True)
                step(n - 1, False)
                dve.wait_ge(S("x_added"), (base + n) * 6 + 6)
                q.link(V.tensor_copy(stat[:, 14:15], C["eps"]), S("moe_done"))
                return n

            steps0 = moe(0, 3, 0)
            norm_apply(2, NC)
            q.do(V.memset(U[:, :, 0, 0:HIST], 0.0))
            q.link(V.memset(U[:, :, 1, 0:HIST - LS], 0.0))
            stream_odd(3, HC)
            dve.wait_ge(S("hist_ready"), KD)
            dve.wait_ge(S("taps_ready"), 2)

            def blocks(x):
                return x.rearrange("p (b l) -> p b l", l=LS)

            def gated(c):
                dve.wait_ge(S("sig_ready"), c + 1)
                q.do(V.scalar_tensor_tensor(U[:, c, :, HIST:], blocks(PS[:, 2 * (c % 4), 0:TOK]), SMT[:, c:c + 1],
                                            blocks(SGC[:, c % 2, :]), ALU.add, ALU.mult), S("u_ready"))

            gated(0)
            for c in range(KD):
                if c + 1 < KD:
                    gated(c + 1)
                dve.wait_ge(S("uhist_ready"), c + 1)
                accs, sides = (blocks(YC[:, c, :]), blocks(YD[:, :])), (S("conv_a"), S("conv_b"))
                for w in range(POOL_TAPS, CONV_W):
                    n = w - POOL_TAPS
                    acc, side = accs[n % 2], sides[n % 2]
                    if side is sides[1] and n < 2 and c:
                        dve.wait_ge(S("conv_sum"), c)
                    if n >= 2:
                        dve.wait_ge(side, q.count[id(side)])
                    src, tap = U[:, c, :, w:w + LS], WDT[:, c, w:w + 1]
                    if n == 0:
                        ins = V.tensor_scalar(acc, src, tap, SMT[:, 16 + c:17 + c], ALU.mult, ALU.add)
                    elif n == 1:
                        ins = V.tensor_scalar(acc, src, tap, None, ALU.mult)
                    else:
                        ins = V.scalar_tensor_tensor(acc, src, tap, acc, ALU.mult, ALU.add)
                    q.do(ins, side)
                q.settle()
                q.link(V.tensor_tensor(YC[:, c, :], YC[:, c, :], YD[:, :], ALU.add), S("conv_sum"))
                dve.wait_ge(S("pool_tap"), (c + 1) * (POOL_TAPS - 1))
                q.do(V.tensor_tensor(YC[:, c, :], YC[:, c, :], YP[:, c % 2, :], ALU.add), S("y_conv"))
            q.settle()
            dve.wait_ge(S("mean_done"), 1)
            for c in range(KD):
                q.do(V.tensor_tensor(YC[:, c, :], YC[:, c, :], PS[:, 6, 0:TOK], ALU.subtract), S("yc_centred"))
            q.settle()
            dve.wait_ge(S("cstd_ready"), 1)
            q.link(V.reciprocal(VR[:, :], VR[:, :]))
            dve.wait_ge(S("ysq_ready"), KD)
            for c in range(KD):
                q.do(V.tensor_tensor(YC[:, c, :], YC[:, c, :], VR[:, :], ALU.mult), S("yc_normed"))
            q.settle()
            add_projection("pw_done", 0)
            moe(1, 5, steps0)


INPUTS = ["x_prompt", "x_sample", "cache_fox_k", "cache_fox_v", "cache_fox_logf", "state_ret", "cache_conv",
          "norm_mix", "norm_ffn", "w_in_mix", "b_forget", "fox_q_gain", "fox_k_gain", "ret_gn_gain", "w_out_mix",
          "w_pw1", "b_pw1", "w_dw", "b_dw", "conv_ln_g", "conv_ln_b", "w_pw2", "w_router_group", "b_router_group",
          "w_router_expert", "b_router_expert", "w_exp_gate", "w_exp_up", "w_exp_down"]
OUTPUTS = [("y_prompt", (1, SEQ, D)), ("y_sample", (NS, LS, D)), ("fox_k_prompt", (1, 1, SEQ, FH, FD)),
           ("fox_v_prompt", (1, 1, SEQ, FH, FD)), ("fox_logf_prompt", (1, 1, SEQ, FH)),
           ("ret_state_prompt", (1, 1, RH, RK, RV)), ("conv_prompt", (1, 1, HIST, D)),
           ("fox_k_sample", (1, NS, LS, FH, FD)), ("fox_v_sample", (1, NS, LS, FH, FD)),
           ("fox_logf_sample", (1, NS, LS, FH)), ("ret_state_sample", (1, NS, RH, RK, RV)),
           ("conv_sample", (1, NS, HIST, D))]


def kernel(**inputs):
    import concourse.bacc as bacc
    from concourse.bass_utils import run_bass_kernel_spmd

    nc = bacc.Bacc("TRN2", target_bir_lowering=False, num_devices=1)
    cst, rcst, head = constants()
    arrays = {name: np.ascontiguousarray(inputs[name]) for name in INPUTS}
    arrays.update(cst=cst, rcst=rcst, head=head)
    a = {name: nc.dram_tensor(f"in_{name}", x.shape, F32, kind="ExternalInput").ap() for name, x in arrays.items()}
    o = {name: nc.dram_tensor(f"out_{name}", shape, F32, kind="ExternalOutput").ap() for name, shape in OUTPUTS}
    build(nc, a, o)
    r = run_bass_kernel_spmd(nc, [{f"in_{name}": x for name, x in arrays.items()}], core_ids=[0])
    return tuple(r.results[0][f"out_{name}"] for name, _ in OUTPUTS)
```
